# Optimizing a Trainium2 kernel written in Bass

```python
import jax
import jax.numpy as jnp
from jax import lax
import numpy as np

D_MODEL = 1024
BATCH = 1
SEQ = 256
DEPTH = 2
DEC_BATCH = 1
DEC_SEQ = 512
PAST_LEN = 128

GRID_W = 64
HEAD_DIM = 64
BRANCH_WIDTH = 256
N_BRANCHES = 4
NA_HEADS = 4
NA_KH_MAX = 8
NA_KW = 16
NA_QBLK_W = 16
NA_KBLK_W = NA_QBLK_W + NA_KW
ML_HEADS = 4
ML_CHUNK = 64
ML_N_GATES = 4
CONV_WIDTH = 31
ATT_Q_HEADS = 4
ATT_KV_HEADS = 2
ATT_GROUP = ATT_Q_HEADS // ATT_KV_HEADS
ATT_QBLK = 128
ROPE_THETA = 10000.0
ROPE_AXIS_DIM = HEAD_DIM // 2
MOE_GROUPS = 4
MOE_EXPERTS_PER_GROUP = 4
MOE_N_EXPERTS = MOE_GROUPS * MOE_EXPERTS_PER_GROUP
MOE_TOP_K = 2
MOE_D_EXPERT = 256
NORM_EPS = 1e-6
NEG_INF = -1e30
F32 = jnp.float32

NA_COLS = 3 * NA_HEADS * HEAD_DIM
ML_COLS = 4 * ML_HEADS * HEAD_DIM + ML_N_GATES * ML_HEADS
CONV_COLS = 2 * BRANCH_WIDTH
ATT_COLS = (ATT_Q_HEADS + 2 * ATT_KV_HEADS) * HEAD_DIM
IN_COLS = NA_COLS + ML_COLS + CONV_COLS + ATT_COLS

kernel_name = 'hybrid_bidir_encoder_na_mlstm_conv_gqa_hmoe'

def rms_norm(x, g):
    xf = x.astype(F32)
    y = xf * lax.rsqrt(jnp.mean(xf * xf, axis=-1, keepdims=True) + NORM_EPS)
    return (y * g.astype(F32)).astype(x.dtype)

def layer_norm(x, g, b):
    xf = x.astype(F32)
    xc = xf - jnp.mean(xf, axis=-1, keepdims=True)
    y = xc * lax.rsqrt(jnp.mean(xc * xc, axis=-1, keepdims=True) + NORM_EPS)
    return (y * g.astype(F32) + b.astype(F32)).astype(x.dtype)

def neighbourhood_attention(q, k, v, rpb):
    bsz, seq = q.shape[0], q.shape[1]
    rows = seq // GRID_W
    kh = min(NA_KH_MAX, rows)
    n_cb = GRID_W // NA_QBLK_W
    r = jnp.arange(rows)
    row_idx = jnp.clip(r - kh // 2, 0, rows - kh)[:, None] + jnp.arange(kh)[None, :]
    cb = jnp.arange(n_cb)
    blk_start = jnp.clip(cb * NA_QBLK_W - NA_KW // 2, 0, GRID_W - NA_KBLK_W)
    key_col = blk_start[:, None] + jnp.arange(NA_KBLK_W)[None, :]
    q_col = cb[:, None] * NA_QBLK_W + jnp.arange(NA_QBLK_W)[None, :]
    win_start = jnp.clip(q_col - NA_KW // 2, 0, GRID_W - NA_KW)
    kc = key_col[:, None, :]
    in_win = (kc >= win_start[..., None]) & (kc < win_start[..., None] + NA_KW)
    col_off = jnp.clip(kc - q_col[..., None] + NA_KW - 1, 0, 2 * NA_KW - 2)
    row_off = row_idx - r[:, None] + NA_KH_MAX - 1
    bias = rpb.astype(F32)[:, row_off][..., col_off]
    bias = jnp.where(in_win[None, None, None], bias, NEG_INF).transpose(0, 1, 3, 4, 2, 5)
    qg = q.reshape(bsz, rows, n_cb, NA_QBLK_W, NA_HEADS, HEAD_DIM)
    kg = k.reshape(bsz, rows, GRID_W, NA_HEADS, HEAD_DIM)
    vg = v.reshape(bsz, rows, GRID_W, NA_HEADS, HEAD_DIM)
    ri = row_idx[:, :, None, None]
    ci = key_col[None, None]
    k_blk = kg[:, ri, ci]
    v_blk = vg[:, ri, ci]
    s = jnp.einsum('brnqhd,brjnkhd->bhrnqjk', qg, k_blk).astype(F32) * HEAD_DIM ** -0.5 + bias[None]
    p = jax.nn.softmax(s.reshape(*s.shape[:-2], -1), axis=-1).reshape(s.shape)
    o = jnp.einsum('bhrnqjk,brjnkhd->brnqhd', p.astype(v.dtype), v_blk)
    return o.reshape(bsz, seq, NA_HEADS * HEAD_DIM)

def mlstm_scan(q, k, v, i_pre, log_f):
    bsz, heads, seq, dh = q.shape
    n_chunks = seq // ML_CHUNK

    def chunks(a):
        return jnp.moveaxis(a.reshape(bsz, heads, n_chunks, ML_CHUNK, *a.shape[3:]), 2, 0)

    causal = jnp.tril(jnp.ones((ML_CHUNK, ML_CHUNK), dtype=bool))

    def step(carry, xs):
        c_mem, n_mem, m_run = carry
        qc, kc, vc, ic, fc = xs
        b = jnp.cumsum(fc, axis=-1)
        log_d = jnp.where(causal, b[..., :, None] - b[..., None, :] + ic[..., None, :], NEG_INF)
        inter = b + m_run[..., None]
        m_row = jnp.maximum(inter, jnp.max(log_d, axis=-1))
        d = jnp.exp(log_d - m_row[..., None])
        w_inter = jnp.exp(inter - m_row)
        s = jnp.einsum('bhld,bhsd->bhls', qc, kc) * d
        num = jnp.einsum('bhls,bhsd->bhld', s, vc) + w_inter[..., None] * jnp.einsum('bhvk,bhlk->bhlv', c_mem, qc)
        den = jnp.sum(s, axis=-1) + w_inter * jnp.einsum('bhk,bhlk->bhl', n_mem, qc)
        h = num / jnp.maximum(jnp.abs(den), jnp.exp(-m_row))[..., None]
        b_end = b[..., -1]
        log_w = b_end[..., None] - b + ic
        m_new = jnp.maximum(b_end + m_run, jnp.max(log_w, axis=-1))
        w = jnp.exp(log_w - m_new[..., None])
        decay = jnp.exp(b_end + m_run - m_new)
        c_new = decay[..., None, None] * c_mem + jnp.einsum('bhl,bhlv,bhlk->bhvk', w, vc, kc)
        n_new = decay[..., None] * n_mem + jnp.einsum('bhl,bhlk->bhk', w, kc)
        return (c_new, n_new, m_new), h

    init = (jnp.zeros((bsz, heads, dh, dh), F32), jnp.zeros((bsz, heads, dh), F32),
            jnp.full((bsz, heads), NEG_INF, F32))
    _, hs = lax.scan(step, init, (chunks(q), chunks(k), chunks(v), chunks(i_pre), chunks(log_f)))
    return jnp.moveaxis(hs, 0, 2).reshape(bsz, heads, seq, dh)

def conformer_conv(u, w_dw, b_dw, g, beta):
    a, gate = jnp.split(u, 2, axis=-1)
    x = a * jax.nn.sigmoid(gate)
    x = lax.conv_general_dilated(x, w_dw[:, None, :].astype(x.dtype), window_strides=(1,),
                                 padding=[(CONV_WIDTH // 2, CONV_WIDTH // 2)],
                                 dimension_numbers=('NWC', 'WIO', 'NWC'),
                                 feature_group_count=BRANCH_WIDTH) + b_dw
    return jax.nn.silu(layer_norm(x, g, beta))

def axial_rope(x, seq):
    t = jnp.arange(seq)
    pos = jnp.stack([t // GRID_W, t % GRID_W], axis=-1).astype(F32)
    inv = ROPE_THETA ** (-jnp.arange(0, ROPE_AXIS_DIM, 2, dtype=F32) / ROPE_AXIS_DIM)
    ang = pos[..., None] * inv
    ang = jnp.concatenate([ang, ang], axis=-1)[:, None]
    xs = x.astype(F32).reshape(*x.shape[:-1], 2, ROPE_AXIS_DIM)
    half = ROPE_AXIS_DIM // 2
    rot = jnp.concatenate([-xs[..., half:], xs[..., :half]], axis=-1)
    return (xs * jnp.cos(ang) + rot * jnp.sin(ang)).reshape(x.shape).astype(x.dtype)

def blocked_gqa(q, k, v):
    bsz, seq = q.shape[0], q.shape[1]
    qb = q.reshape(bsz, seq // ATT_QBLK, ATT_QBLK, ATT_KV_HEADS, ATT_GROUP, HEAD_DIM).transpose(1, 0, 2, 3, 4, 5)

    def one_block(q_blk):
        s = jnp.einsum('bqhgd,bkhd->bhgqk', q_blk, k).astype(F32) * HEAD_DIM ** -0.5
        p = jax.nn.softmax(s, axis=-1).astype(v.dtype)
        return jnp.einsum('bhgqk,bkhd->bqhgd', p, v)

    o = lax.map(one_block, qb)
    return o.transpose(1, 0, 2, 3, 4, 5).reshape(bsz, seq, ATT_Q_HEADS * HEAD_DIM)

def hybrid_mixer(h, w_in, na_rpb, ml_gate_b, ml_norm_g, conv_dw_w, conv_dw_b, conv_norm_g, conv_norm_b,
                 att_q_norm_g, att_k_norm_g, w_branch, w_gate, b_gate, w_out):
    bsz, seq, _ = h.shape
    u = jnp.einsum('bsd,dc->bsc', h, w_in)
    u_na, u_ml, u_cv, u_at = jnp.split(u, [NA_COLS, NA_COLS + ML_COLS, NA_COLS + ML_COLS + CONV_COLS], axis=-1)

    qkv_a = u_na.reshape(bsz, seq, 3, NA_HEADS, HEAD_DIM)
    o_na = neighbourhood_attention(qkv_a[:, :, 0], qkv_a[:, :, 1], qkv_a[:, :, 2], na_rpb)

    qkvo = u_ml[..., :4 * BRANCH_WIDTH].reshape(bsz, seq, 4, ML_HEADS, HEAD_DIM)
    gates = u_ml[..., 4 * BRANCH_WIDTH:].reshape(bsz, seq, ML_N_GATES, ML_HEADS).astype(F32) + ml_gate_b.astype(F32)
    gates = gates.transpose(2, 0, 3, 1)
    qm = qkvo[:, :, 0].astype(F32).transpose(0, 2, 1, 3)
    km = qkvo[:, :, 1].astype(F32).transpose(0, 2, 1, 3) * HEAD_DIM ** -0.5
    vm = qkvo[:, :, 2].astype(F32).transpose(0, 2, 1, 3)
    h_fwd = mlstm_scan(qm, km, vm, gates[0], jax.nn.log_sigmoid(gates[1]))
    h_bwd = jnp.flip(mlstm_scan(jnp.flip(qm, 2), jnp.flip(km, 2), jnp.flip(vm, 2),
                                jnp.flip(gates[2], 2), jnp.flip(jax.nn.log_sigmoid(gates[3]), 2)), 2)
    hm = rms_norm((h_fwd + h_bwd).transpose(0, 2, 1, 3), ml_norm_g.reshape(ML_HEADS, HEAD_DIM))
    o_ml = (hm * jax.nn.sigmoid(qkvo[:, :, 3].astype(F32))).reshape(bsz, seq, BRANCH_WIDTH).astype(h.dtype)

    o_cv = conformer_conv(u_cv, conv_dw_w, conv_dw_b, conv_norm_g, conv_norm_b)

    nq = ATT_Q_HEADS * HEAD_DIM
    nk = ATT_KV_HEADS * HEAD_DIM
    qd = u_at[..., :nq].reshape(bsz, seq, ATT_Q_HEADS, HEAD_DIM)
    kd = u_at[..., nq:nq + nk].reshape(bsz, seq, ATT_KV_HEADS, HEAD_DIM)
    vd = u_at[..., nq + nk:].reshape(bsz, seq, ATT_KV_HEADS, HEAD_DIM)
    qd = axial_rope(rms_norm(qd, att_q_norm_g), seq)
    kd = axial_rope(rms_norm(kd, att_k_norm_g), seq)
    o_at = blocked_gqa(qd, kd, vd)

    branches = jnp.stack([o_na, o_ml.astype(o_na.dtype), o_cv.astype(o_na.dtype), o_at.astype(o_na.dtype)], axis=2)
    proj = jnp.einsum('bsnc,ncd->bsnd', branches, w_branch).astype(F32)
    g = jax.nn.sigmoid((jnp.einsum('bsd,dc->bsc', h, w_gate) + b_gate).astype(F32)).reshape(bsz, seq, N_BRANCHES, D_MODEL)
    merged = jnp.sum(g * proj, axis=2).astype(h.dtype)
    return jnp.einsum('bsd,de->bse', merged, w_out)

def hierarchical_moe(h, w_group, b_group, w_expert, b_expert, w1, w3, w2):
    g_logits = (jnp.einsum('bsd,dg->bsg', h, w_group) + b_group).astype(F32)
    g_prob = jax.nn.softmax(g_logits, axis=-1)
    g_idx = jnp.argmax(g_logits, axis=-1)
    g_gate = jnp.take_along_axis(g_prob, g_idx[..., None], axis=-1)[..., 0]
    e_logits = (jnp.einsum('bsd,dge->bsge', h, w_expert) + b_expert).astype(F32)
    e_in = jnp.take_along_axis(e_logits, g_idx[..., None, None], axis=2)[..., 0, :]
    top_val, top_idx = lax.top_k(e_in, MOE_TOP_K)
    top_w = jax.nn.softmax(top_val, axis=-1) * g_gate[..., None]
    expert_id = g_idx[..., None] * MOE_EXPERTS_PER_GROUP + top_idx
    combine = jnp.sum(jax.nn.one_hot(expert_id, MOE_N_EXPERTS, dtype=F32) * top_w[..., None], axis=-2)
    a = jnp.einsum('bsd,edf->bsef', h, w1)
    b = jnp.einsum('bsd,edf->bsef', h, w3)
    hid = jax.nn.silu(a) * b * combine[..., None].astype(h.dtype)
    return jnp.einsum('bsef,efd->bsd', hid, w2)

def encoder_trunk(x, norm_mix_g, w_in, na_rpb, ml_gate_b, ml_norm_g, conv_dw_w, conv_dw_b, conv_norm_g,
                  conv_norm_b, att_q_norm_g, att_k_norm_g, w_branch, w_gate, b_gate, w_out, norm_ffn_g,
                  moe_w_group, moe_b_group, moe_w_expert, moe_b_expert, moe_w1, moe_w3, moe_w2, final_norm_g):
    for l in range(DEPTH):
        h = rms_norm(x, norm_mix_g[l])
        x = x + hybrid_mixer(h, w_in[l], na_rpb[l], ml_gate_b[l], ml_norm_g[l], conv_dw_w[l], conv_dw_b[l],
                             conv_norm_g[l], conv_norm_b[l], att_q_norm_g[l], att_k_norm_g[l], w_branch[l],
                             w_gate[l], b_gate[l], w_out[l]).astype(x.dtype)
        h = rms_norm(x, norm_ffn_g[l])
        x = x + hierarchical_moe(h, moe_w_group[l], moe_b_group[l], moe_w_expert[l], moe_b_expert[l],
                                 moe_w1[l], moe_w3[l], moe_w2[l]).astype(x.dtype)
    return rms_norm(x, final_norm_g)

def setup_inputs(seed: int = 0) -> dict:
    key = jax.random.key(seed)
    ks = jax.random.split(key, 26)

    def nrm(k, shape, scale):
        return jax.random.normal(k, shape, F32) * scale

    L, D = DEPTH, D_MODEL
    f_base = jnp.array([0.0, 1.0, 0.0, 1.0], F32)[:, None] * jnp.linspace(3.0, 6.0, ML_HEADS, dtype=F32)[None, :]
    return {
        'x_prompt': nrm(ks[0], (BATCH, SEQ, D), 1.0),
        'x_sample': nrm(ks[1], (DEC_BATCH, DEC_SEQ, D), 1.0),
        'norm_mix_g': 1.0 + nrm(ks[2], (L, D), 0.05),
        'w_in': nrm(ks[3], (L, D, IN_COLS), D ** -0.5),
        'na_rpb': nrm(ks[4], (L, NA_HEADS, 2 * NA_KH_MAX - 1, 2 * NA_KW - 1), 0.2),
        'ml_gate_b': f_base[None] + nrm(ks[5], (L, ML_N_GATES, ML_HEADS), 0.1),
        'ml_norm_g': 1.0 + nrm(ks[6], (L, BRANCH_WIDTH), 0.05),
        'conv_dw_w': nrm(ks[7], (L, CONV_WIDTH, BRANCH_WIDTH), CONV_WIDTH ** -0.5),
        'conv_dw_b': nrm(ks[8], (L, BRANCH_WIDTH), 0.02),
        'conv_norm_g': 1.0 + nrm(ks[9], (L, BRANCH_WIDTH), 0.05),
        'conv_norm_b': nrm(ks[10], (L, BRANCH_WIDTH), 0.02),
        'att_q_norm_g': 1.0 + nrm(ks[11], (L, HEAD_DIM), 0.05),
        'att_k_norm_g': 1.0 + nrm(ks[12], (L, HEAD_DIM), 0.05),
        'w_branch': nrm(ks[13], (L, N_BRANCHES, BRANCH_WIDTH, D), BRANCH_WIDTH ** -0.5),
        'w_gate': nrm(ks[14], (L, D, N_BRANCHES * D), D ** -0.5),
        'b_gate': nrm(ks[15], (L, N_BRANCHES * D), 0.02),
        'w_out': nrm(ks[16], (L, D, D), D ** -0.5),
        'norm_ffn_g': 1.0 + nrm(ks[17], (L, D), 0.05),
        'moe_w_group': nrm(ks[18], (L, D, MOE_GROUPS), D ** -0.5),
        'moe_b_group': nrm(ks[19], (L, MOE_GROUPS), 0.01),
        'moe_w_expert': nrm(ks[20], (L, D, MOE_GROUPS, MOE_EXPERTS_PER_GROUP), D ** -0.5),
        'moe_b_expert': nrm(ks[21], (L, MOE_GROUPS, MOE_EXPERTS_PER_GROUP), 0.01),
        'moe_w1': nrm(ks[22], (L, MOE_N_EXPERTS, D, MOE_D_EXPERT), D ** -0.5),
        'moe_w3': nrm(ks[23], (L, MOE_N_EXPERTS, D, MOE_D_EXPERT), D ** -0.5),
        'moe_w2': nrm(ks[24], (L, MOE_N_EXPERTS, MOE_D_EXPERT, D), MOE_D_EXPERT ** -0.5),
        'final_norm_g': 1.0 + nrm(ks[25], (D,), 0.05),
    }

def reference(x_prompt, x_sample, norm_mix_g, w_in, na_rpb, ml_gate_b, ml_norm_g, conv_dw_w, conv_dw_b,
              conv_norm_g, conv_norm_b, att_q_norm_g, att_k_norm_g, w_branch, w_gate, b_gate, w_out, norm_ffn_g,
              moe_w_group, moe_b_group, moe_w_expert, moe_b_expert, moe_w1, moe_w3, moe_w2, final_norm_g):
    y_prompt = encoder_trunk(x_prompt, norm_mix_g, w_in, na_rpb, ml_gate_b, ml_norm_g, conv_dw_w, conv_dw_b,
                             conv_norm_g, conv_norm_b, att_q_norm_g, att_k_norm_g, w_branch, w_gate, b_gate,
                             w_out, norm_ffn_g, moe_w_group, moe_b_group, moe_w_expert, moe_b_expert, moe_w1,
                             moe_w3, moe_w2, final_norm_g)
    y_sample = encoder_trunk(x_sample, norm_mix_g, w_in, na_rpb, ml_gate_b, ml_norm_g, conv_dw_w, conv_dw_b,
                             conv_norm_g, conv_norm_b, att_q_norm_g, att_k_norm_g, w_branch, w_gate, b_gate,
                             w_out, norm_ffn_g, moe_w_group, moe_b_group, moe_w_expert, moe_b_expert, moe_w1,
                             moe_w3, moe_w2, final_norm_g)
    return (y_prompt, y_sample)


_drawn_inputs = setup_inputs


def setup_inputs(seed=0):
    import zlib

    import numpy as np

    out = dict(_drawn_inputs(seed))
    spreads = {}
    factors = {'att_q_norm_g': 3.236, 'att_k_norm_g': 6.753, 'moe_b_group': 3.168, 'moe_b_expert': 3.609}
    for name, (base, spread) in spreads.items():
        noise = np.random.default_rng([zlib.crc32(name.encode()), seed]).standard_normal(out[name].shape)
        drawn = base * np.exp(spread * noise) if base else spread * noise
        out[name] = jnp.asarray(drawn.astype(out[name].dtype))
    for name, factor in factors.items():
        out[name] = (out[name] * factor).astype(out[name].dtype)
    return out
```

```python
from contextlib import ExitStack

import numpy as np

import concourse.bass as bass
from concourse import mybir

F32 = mybir.dt.float32
ALU = mybir.AluOpType
ACT = mybir.ActivationFunctionType
AX = mybir.AxisListType

P = 128
D = 1024
KD = D // P
L = 2
GROUPS = [(0, 2), (2, 4)]
T = sum(n for _, n in GROUPS)
TOK = T * P
HALF = TOK // 2
GRID = 64
HD = 64
BW = 256
HEADS = 4
TAPS = 31
PAD = TAPS // 2
NBR = 4
NG = 4
NE = 16
DE = 256
EPS = 1e-6
NEG = -1e30
CHUNKS = 16
MIX_CHUNKS = 6
CW = KD * 512
EW = KD * 2 * DE + 2 * D
SEGS = [(0, 256, 0), (256, 512, 256 + PAD)]
CONV_OUT = TOK + PAD
CONV_IN = TOK + 3 * PAD
ATT_UNITS = T * HEADS

PP_GMIX, PP_GFFN, PP_CW, PP_CB, PP_GB, PP_BG = 0, 8, 16, 78, 80, 81
PP_N = 113
R_ATT, R_ML, R_CG, R_CB, R_MOE = 0, 384, 640, 896, 1152
R_N = 1172
C_ID, C_COS, C_SIN, C_WIN, C_TRI, C_SEL, C_IOTA = 0, 128, 512, 896, 960, 1216, 2240
C_N = 2244


class Tally:

    def __init__(self, eng, chain):
        self.eng, self.chain, self.n = eng, chain, {}

    def __call__(self, ins, sem=None):
        sem = self.chain if sem is None else sem
        ins.then_inc(sem, 1)
        self.n[sem.num] = self.n.get(sem.num, 0) + 1
        self.eng.wait_ge(sem, self.n[sem.num])


def tile_group(tile):
    return 0 if tile < GROUPS[0][1] else 1


PROJ_UNITS = {"cv": 8, "at": 6, "na": 8, "nv": 6, "ml": 8, "mo": 6, "mg": 2}
CHUNK_OF = {"cv": 0, "at": 1, "na": 2, "nv": 3, "ml": 4, "mo": 5, "mg": 5}


def schedule():
    steps, count, at = [], {}, {}

    def add(kind, *key):
        i = count.get(kind, 0)
        count[kind] = i + 1
        at[(kind, *key)] = i
        steps.append((kind, i, key))

    def proj(name):
        for u in range(PROJ_UNITS[name]):
            add("proj", name, u)

    def attention(name, extra=None):
        units = [(tile, h) for tile in range(T) for h in range(HEADS)]
        add("score", name, *units[0])
        for i, (tile, h) in enumerate(units):
            if i + 1 < len(units):
                add("score", name, *units[i + 1])
            if extra:
                add(extra)
            add("attend", name, tile, h)
            if h == HEADS - 1:
                add("turn", name, tile)

    def turns(name):
        for t in range(T):
            add("turn", name, t)

    proj("cv")
    proj("at")
    add("glu")
    add("rope")
    turns("qk")
    attention("at", "conv")
    turns("cy")
    add("cnorm")
    turns("cv")
    add("bias")
    for name in ("na", "nv", "ml", "mo", "mg"):
        proj(name)
    add("gates")
    turns("am")
    attention("na")
    for h in range(HEADS):
        for g in range(len(GROUPS)):
            add("ml", g, h)
    add("mnorm")
    turns("ml")
    return steps, at


def program(nc, x_prompt, x_sample, wd, wb, we, wr, pp_in, rows_in, fin_in, bias_in, consts_in, y_prompt, y_sample):
    steps, at = schedule()
    units_of = {}
    for kind, i, key in steps:
        units_of[kind] = i + 1
    last_proj = {}
    for kind, i, key in steps:
        if kind == "proj":
            last_proj[CHUNK_OF[key[0]]] = i
    attends = [key for kind, i, key in steps if kind == "attend"]
    tt, ts_, stt = nc.vector.tensor_tensor, nc.vector.tensor_scalar, nc.vector.scalar_tensor_tensor
    reduce_, scan, activate = nc.vector.tensor_reduce, nc.vector.tensor_tensor_scan, nc.scalar.activation

    ctx = ExitStack()
    with ctx:
        def sb(name, shape):
            return ctx.enter_context(nc.sbuf_tensor(name, shape, F32))

        def once(name):
            return ctx.enter_context(nc.semaphore(name))

        layer_sems = []

        def sem(name):
            s = ctx.enter_context(nc.semaphore(name))
            layer_sems.append(s.num)
            return s

        x = sb("x", [P, T, D])
        hT = sb("hT", [P, KD, TOK])
        ring = sb("ring", [P, 2, CW])
        wide = sb("wide", [P, CW])
        reg_a = sb("reg_a", [P, 4608])
        reg_b = sb("reg_b", [P, 6200])
        oT = sb("oT", [P, 8, TOK])
        cvx = sb("cvx", [P, 2, CONV_IN])
        consts = sb("consts", [P, C_N])
        rows = sb("rows", [P, R_N])
        pp = sb("pp", [P, PP_N])
        prob = sb("prob", [P, 2, 512])
        probT = sb("probT", [P, 2, 512])
        outb = sb("outb", [P, 2, BW])
        am_rows = sb("am_rows", [P, TOK])
        dg = sb("dg", [P, 512])
        ones = sb("ones", [P, 512])
        wr_sb = sb("wr_sb", [P, KD, NG + NE])
        small = sb("small", [P, 1024])

        ident = consts[:, C_ID:C_ID + P]
        cos = consts[:, C_COS:C_COS + 384].rearrange("p (t d) -> p t d", t=T)
        sin = consts[:, C_SIN:C_SIN + 384].rearrange("p (t d) -> p t d", t=T)
        win = consts[:, C_WIN:C_WIN + GRID]
        tri = consts[:, C_TRI:C_TRI + 256].rearrange("p (d t) -> p d t", d=2)
        sel = consts[:, C_SEL:C_SEL + 1024].rearrange("p (j m) -> p j m", j=8)
        iota4 = consts[:, C_IOTA:C_IOTA + 4]

        cvag = reg_a[:, 0:4 * TOK].rearrange("p (j t) -> p j t", j=4)
        cvy = reg_a[:, 0:2 * CONV_OUT].rearrange("p (j t) -> p j t", j=2)
        cvz = reg_a[:, 3072:4608].rearrange("p (t c) -> p t c", t=T)
        naqk = reg_a[:, 0:4 * TOK].rearrange("p (j t) -> p j t", j=4)
        nav = reg_a[:, 3072:4608].rearrange("p (t c) -> p t c", t=T)
        hm = reg_a[:, 0:1536].rearrange("p (t c) -> p t c", t=T)
        atr = reg_b[:, 0:3072].rearrange("p (t c) -> p t c", t=T)
        att = reg_b[:, 3072:5376].rearrange("p (j t) -> p j t", j=3)
        mlqk = reg_b[:, 0:3072].rearrange("p (j t) -> p j t", j=4)
        mlv = reg_b[:, 3072:4632].rearrange("p (t h c) -> p t h c", t=T, h=HEADS)
        mlo = reg_b[:, 4632:6168].rearrange("p (t c) -> p t c", t=T)
        mT = reg_b[:, 0:KD * TOK].rearrange("p (k t) -> p k t", k=KD)
        rope_tmp = oT[:, 0:3, :].rearrange("p a (b c) -> p (a b) c", c=384)
        cvt = oT[:, 0:2, :].rearrange("p a (b c) -> p (a b) c", c=BW)
        top_rows, sum_rows = oT[:, 2, :], oT[:, 3, :]
        bias_tab = wide[:, :].rearrange("p (h r c) -> p h r c", h=HEADS, r=16)
        mlw = wide[:, :].rearrange("p (d j t) -> p d j t", d=2, j=4)
        tanh_buf = [prob[:, 0, 0:HALF], prob[:, 1, 0:HALF], probT[:, 0, 0:HALF], probT[:, 1, 0:HALF]]
        slot_w = [oT[:, :, :].rearrange("p a b -> p (a b)")[:, 0:EW], reg_b[:, 0:EW]]

        msq, rstd, nhalf = small[:, 0:64], small[:, 64:128], small[:, 128:192]
        negm, rsum, rrec = small[:, 192:194], small[:, 194:196], small[:, 196:197]
        am = small[:, 200:248].rearrange("p (t d h) -> p t d h", t=T, d=2)
        em = small[:, 248:296].rearrange("p (t d h) -> p t d h", t=T, d=2)
        den = small[:, 296:304].rearrange("p (d t) -> p d t", d=2)
        den2 = small[:, 304:312].rearrange("p (d t) -> p d t", d=2)
        lmean = small[:, 312:318]
        bg_half = small[:, 320:352]
        rt = small[:, 352:1024]
        comb = small[:, 928:1024].rearrange("p (t e) -> p t e", t=T)

        bank = [ctx.enter_context(nc.psum_tensor(f"bank{i}", [P, 512], F32)) for i in range(8)]

        inputs_in, setup_done, stored = once("inputs_in"), once("setup_done"), [once("stored0"), once("stored1")]
        chunk_in = [sem("chunk_in0"), sem("chunk_in1")]
        params_in, bias_in_sem, wb_in, wr_in = sem("params_in"), sem("bias_in"), sem("wb_in"), sem("wr_in")
        expert_in = [sem("expert_in0"), sem("expert_in1")]
        proj_mm, turn_mm, score_mm, pt_mm, pv_mm = (sem("proj_mm"), sem("turn_mm"), sem("score_mm"), sem("pt_mm"),
                                                    sem("pv_mm"))
        decay_mm, mlpv_mm = sem("decay_mm"), sem("mlpv_mm")
        a_mix, proj_ev, turn_ev, exp_done, pt_ev = (sem("a_mix"), sem("proj_ev"), sem("turn_ev"), sem("exp_done"),
                                                    sem("pt_ev"))
        ctanh_done, lsig_ln, decay_done = sem("ctanh_done"), sem("lsig_ln"), sem("decay_done")
        v_mix, glu_done, rope_done, conv_done, cz_done, cn_done = (
            sem("v_mix"), sem("glu_done"), sem("rope_done"), sem("conv_done"), sem("cz_done"), sem("cn_done"))
        max_done, head_done, score_free, bias_done = sem("max_done"), sem("head_done"), sem("score_free"), sem("bias_done")
        lsig_min, rows_done, masked, mlh_done, mn_done = (sem("lsig_min"), sem("rows_done"), sem("masked"),
                                                          sem("mlh_done"), sem("mn_done"))
        mix_var, mix_rs = sem("mix_var"), sem("mix_rs")
        v_merge, bgh_done, gate_mm, branch_mm, tanh_done = (sem("v_merge"), sem("bgh_done"), sem("gate_mm"),
                                                            sem("branch_mm"), sem("tanh_done"))
        gated, merged, out_mm, out_ev = sem("gated"), sem("merged"), sem("out_mm"), sem("out_ev")
        v_route, route_mm, route_diff, route_exp, comb_done = (
            sem("v_route"), sem("route_mm"), sem("route_diff"), sem("route_exp"), sem("comb_done"))
        v_exp, up_mm, th_done, hid_done, hid_mm, hid_ev = (sem("v_exp"), sem("up_mm"), sem("th_done"), sem("hid_done"),
                                                           sem("hid_mm"), sem("hid_ev"))
        down_mm, y_ev = sem("down_mm"), sem("y_ev")

        with nc.Block() as block:
            @block.sync
            def _(sp):
                sp.dma_start(consts[:, :], consts_in).then_inc(inputs_in, 16)
                sp.dma_start(x[:, 0:2, :], x_prompt.rearrange("b (t p) d -> p (b t) d", p=P)).then_inc(inputs_in, 16)
                sp.dma_start(x[:, 2:6, :], x_sample.rearrange("b (t p) d -> p (b t) d", p=P)).then_inc(inputs_in, 16)
                sp.wait_ge(inputs_in, 48)

            @block.gpsimd
            def _(pool):
                pool.memset(nhalf, -0.5).then_inc(setup_done, 1)
                pool.memset(ones[:, :], 1.0).then_inc(setup_done, 1)
                pool.memset(cvx[:, :, :], 0.0).then_inc(setup_done, 1)
                pool.wait_ge(setup_done, 3)

        def normalised(name, read_params, turned, register):
            a_chain, sq_done, var_done, rs_done, h_done, ht_mm, ht_ev = (
                register(f"{name}_{s}") for s in ("chain", "sq", "var", "rs", "h", "ht_mm", "ht_ev"))
            hb = reg_a[:, 0:2 * D].rearrange("p (s d) -> p s d", s=2)
            squares = reg_a[:, 2 * D:3 * D]
            gain_row = reg_a[:, 3 * D:4 * D]
            with nc.Block() as block:
                @block.sync
                def _(sp):
                    read_params(sp)
                    if turned is None:
                        for t in range(T):
                            sp.wait_ge(h_done, t + 1)
                            y, r = (y_prompt, t) if t < 2 else (y_sample, t - 2)
                            sp.dma_start(y[0, r * P:(r + 1) * P, :], hb[:, t % 2, :]).then_inc(stored[t % 2], 16)
                        for s in range(2):
                            sp.wait_ge(stored[s], 16 * (T // 2))

                @block.scalar
                def _(act):
                    done = Tally(act, a_chain)
                    for t in range(T):
                        done(activate(squares, x[:, t, :], ACT.Square, accum_out=msq[:, t:t + 1]),
                             sq_done if t == T - 1 else a_chain)

                @block.gpsimd
                def _(pool):
                    pool.wait_ge(var_done, 1)
                    nc.gpsimd.tensor_tensor(rstd[:, 0:T], msq[:, 8:8 + T], nhalf[:, 0:T], ALU.pow).then_inc(rs_done, 1)

                @block.vector
                def _(dve):
                    dve.wait_ge(sq_done, 1)
                    ts_(msq[:, 8:8 + T], msq[:, 0:T], 1.0 / D, EPS, ALU.mult, ALU.add).then_inc(var_done, 1)
                    dve.wait_ge(rs_done, 1)
                    dve.wait_ge(params_in if turned is not None else inputs_in, 32 if turned is not None else 64)

                    def scale(t):
                        if t >= 2 and turned is not None:
                            dve.wait_ge(ht_mm, 2 * (t - 1))
                        if t >= 2 and turned is None:
                            dve.wait_ge(stored[t % 2], 16 * (t // 2))
                        if turned is None:
                            stt(hb[:, t % 2, :], x[:, t, :], rstd[:, t:t + 1], gain_row, ALU.mult,
                                ALU.mult).then_inc(h_done, 1)
                        else:
                            ts_(hb[:, t % 2, :], x[:, t, :], rstd[:, t:t + 1], None, ALU.mult).then_inc(h_done, 1)

                    scale(0)
                    for t in range(T):
                        if t + 1 < T:
                            scale(t + 1)
                        for q in range(2 if turned is not None else 0):
                            dve.wait_ge(ht_mm, 2 * t + q + 1)
                            tt(hT[:, 4 * q:4 * q + 4, t * P:(t + 1) * P],
                               bank[(2 * t + q) % 4][:, :].rearrange("p (k c) -> p k c", k=4),
                               pp[:, turned + 4 * q:turned + 4 * q + 4].unsqueeze(2).to_broadcast([P, 4, P]),
                               ALU.mult).then_inc(ht_ev, 1)

                if turned is None:
                    return

                @block.tensor
                def _(pe):
                    for t in range(T):
                        pe.wait_ge(h_done, t + 1)
                        for q in range(2):
                            if t >= 2:
                                pe.wait_ge(ht_ev, 2 * t + q - 3)
                            for k in range(4):
                                mm = nc.tensor.transpose(bank[(2 * t + q) % 4][:, k * P:(k + 1) * P],
                                                         hb[:, t % 2, (4 * q + k) * P:(4 * q + k + 1) * P], ident)
                            mm.then_inc(ht_mm, 1)

        def load_chunk(sp, layer, c):
            sp.dma_start(ring[:, c % 2, :], wd[bass.ds(layer * CHUNKS + c, 1)].rearrange("a p n -> (a p) n")
                         ).then_inc(chunk_in[c % 2], 16)

        def wait_chunk(pe, c):
            pe.wait_ge(chunk_in[c % 2], 16 * (c // 2 + 1))

        def score_bank(pe, s):
            if s >= 2:
                if s - 2 < ATT_UNITS:
                    pe.wait_ge(exp_done, s - 1)
                else:
                    pe.wait_ge(score_free, s - 1 - ATT_UNITS)

        def mix_tensor(pe):
            def proj(i, name, u):
                c = CHUNK_OF[name]
                w = ring[:, c % 2, :].rearrange("p (k n) -> p k n", k=KD)
                wait_chunk(pe, c)
                if i >= 2:
                    pe.wait_ge(proj_ev, i - 1)
                for k in range(KD):
                    st = dict(start=(k == 0), stop=(k == KD - 1))
                    if name in ("cv", "na", "ml", "mg"):
                        j, hf = (u // 2, u % 2) if name != "mg" else (2, u)
                        mm = nc.tensor.matmul(bank[i % 2][:, 0:HALF], w[:, k, j * P:(j + 1) * P],
                                              hT[:, k, hf * HALF:(hf + 1) * HALF], **st)
                    else:
                        n = BW if name == "mo" else 512
                        mm = nc.tensor.matmul(bank[i % 2][:, 0:n], hT[:, k, u * P:(u + 1) * P], w[:, k, 0:n], **st)
                mm.then_inc(proj_mm, 1)

            def score(i, name, tile, h):
                first, n = GROUPS[tile_group(tile)]
                tq, tk = slice(tile * P, (tile + 1) * P), slice(first * P, (first + n) * P)
                score_bank(pe, i)
                if name == "at":
                    pe.wait_ge(turn_ev, at[("turn", "qk", first + n - 1)] + 1)
                    part = slice(HD * (h // 2), HD * (h // 2) + HD)
                    q, k = att[part, h % 2, tq], att[part, 2, tk]
                else:
                    pe.wait_ge(proj_ev, at[("proj", "nv", T - 1)] + 1)
                    part = slice(HD * (h % 2), HD * (h % 2) + HD)
                    q, k = naqk[part, h // 2, tq], naqk[part, 2 + h // 2, tk]
                nc.tensor.matmul(bank[4 + i % 2][:, 0:n * P], q, k, start=True, stop=True).then_inc(score_mm, 1)

            def attend(i, name, tile, h):
                first, n = GROUPS[tile_group(tile)]
                pe.wait_ge(exp_done, i + 1)
                if i >= 1:
                    pe.wait_ge(pt_ev, i)
                for k in range(n):
                    mm = nc.tensor.transpose(bank[6][:, k * P:(k + 1) * P], prob[:, i % 2, k * P:(k + 1) * P], ident)
                mm.then_inc(pt_mm, 1)
                pe.wait_ge(pt_ev, i + 1)
                if i >= 1:
                    pe.wait_ge(head_done, i)
                for k in range(n):
                    v = (atr[:, first + k, 384 + HD * (h // 2):384 + HD * (h // 2) + HD] if name == "at"
                         else nav[:, first + k, HD * h:HD * h + HD])
                    mm = nc.tensor.matmul(bank[7][:, HD * h:HD * h + HD], probT[:, i % 2, k * P:(k + 1) * P],
                                          v, start=(k == 0), stop=(k == n - 1))
                mm.then_inc(pv_mm, 1)

            def turn(i, name, t):
                if i >= 1:
                    pe.wait_ge(turn_ev, i)
                if name == "qk":
                    pe.wait_ge(rope_done, 1)
                    parts = [atr[:, t, j * P:(j + 1) * P] for j in range(3)]
                elif name == "cy":
                    pe.wait_ge(conv_done, 1)
                    first, _, off = SEGS[tile_group(t)]
                    o = off + t * P - first
                    parts = [cvy[:, j, o:o + P] for j in range(2)]
                elif name == "am":
                    pe.wait_ge(rows_done, 1)
                    parts = [am_rows[:, t * P:(t + 1) * P]]
                else:
                    if name == "cv":
                        pe.wait_ge(cn_done, 1)
                        o = cvz[:, t, :]
                    elif name == "ml":
                        pe.wait_ge(mn_done, 1)
                        o = hm[:, t, :]
                    else:
                        pe.wait_ge(head_done, at[("attend", name, t, HEADS - 1)] + 1)
                        o = outb[:, t % 2, :]
                    parts = [o[:, 0:P], o[:, P:BW]]
                for j, part in enumerate(parts):
                    mm = nc.tensor.transpose(bank[3][:, j * P:(j + 1) * P], part, ident)
                mm.then_inc(turn_mm, 1)

            s_next = units_of["score"]

            def ml(i, g, h):
                nonlocal s_next
                first, n = GROUPS[g]
                tk = slice(first * P, (first + n) * P)
                pe.wait_ge(rows_done, 1)
                pe.wait_ge(proj_ev, units_of["proj"])
                for d in range(2):
                    if i or d:
                        pe.wait_ge(decay_done, 2 * i + d)
                    nc.tensor.matmul(bank[2][:, 0:n * P], sel[0:64, 4 * d + h, :], top_rows[0:64, tk],
                                     start=True, stop=True).then_inc(decay_mm, 1)
                part = slice(HD * (h % 2), HD * (h % 2) + HD)
                for j in range(n):
                    score_bank(pe, s_next)
                    nc.tensor.matmul(bank[4 + s_next % 2][:, 0:n * P],
                                     mlqk[part, 2 + h // 2, (first + j) * P:(first + j + 1) * P],
                                     mlqk[part, h // 2, tk], start=True, stop=True).then_inc(score_mm, 1)
                    s_next += 1
                pe.wait_ge(score_free, s_next - ATT_UNITS)
                if i == 0:
                    pe.wait_ge(pt_ev, units_of["attend"])
                    pe.wait_ge(head_done, units_of["attend"])
                else:
                    pe.wait_ge(mlh_done, i)
                for d in range(2):
                    for t in range(n):
                        js = range(t + 1) if d == 0 else range(t, n)
                        for j in js:
                            mm = nc.tensor.matmul(bank[6 + d][:, 65 * t:65 * t + 65], mlw[:, d, j, t * P:(t + 1) * P],
                                                  mlv[:, first + j, h, :], start=(j == js[0]), stop=(j == js[-1]))
                mm.then_inc(mlpv_mm, 1)

            for kind, i, key in steps:
                if kind in ("proj", "score", "attend", "turn", "ml"):
                    {"proj": proj, "score": score, "attend": attend, "turn": turn, "ml": ml}[kind](i, *key)

        def mix_scalar(act):
            done = Tally(act, a_mix)
            at_over = at[("attend", "at", T - 1, HEADS - 1)] + 1

            def proj(i, name, u):
                b, half, j = bank[i % 2], slice((u % 2) * HALF, (u % 2 + 1) * HALF), u // 2
                act.wait_ge(proj_mm, i + 1)
                if name == "na" and u == 0:
                    act.wait_ge(turn_mm, at[("turn", "cv", T - 1)] + 1)
                if name in ("nv", "ml") and u == 0:
                    act.wait_ge(pv_mm, at_over)
                if name == "cv" and j < 2:
                    ins = activate(cvag[:, j, half], b[:, 0:HALF], ACT.Copy, scale=0.5)
                elif name == "cv":
                    ins = activate(cvag[:, j, half], b[:, 0:HALF], ACT.Tanh, scale=0.5)
                elif name == "na":
                    ins = activate(naqk[:, j, half], b[:, 0:HALF], ACT.Copy, scale=HD ** -0.5 if j < 2 else 1.0)
                elif name == "ml":
                    ins = activate(mlqk[:, j, half], b[:, 0:HALF], ACT.Copy, scale=1.0 if j < 2 else HD ** -0.5)
                elif name == "mg":
                    ins = activate(top_rows[:, half], b[:, 0:HALF], ACT.Identity, bias=pp[:, PP_GB:PP_GB + 1])
                elif name == "at":
                    ins = activate(atr[:, u, :], b[:, :], ACT.Copy)
                elif name == "mo":
                    ins = activate(mlo[:, u, :], b[:, 0:BW], ACT.Tanh, scale=0.5)
                else:
                    done(activate(nav[:, u, :], b[:, 0:BW], ACT.Copy))
                    done(activate(mlv[:, u, :, HD], ones[:, 0:HEADS], ACT.Copy))
                    ins = activate(mlv[:, u, :, 0:HD], b[:, BW:2 * BW].rearrange("p (h c) -> p h c", h=HEADS), ACT.Copy)
                done(ins, proj_ev)

            def attend(i, name, tile, h):
                S = GROUPS[tile_group(tile)][1] * P
                act.wait_ge(max_done, i + 1)
                if i >= 2:
                    act.wait_ge(pt_mm, i - 1)
                    act.wait_ge(head_done, i - 1)
                src = bank[4 + i % 2][:, 0:S] if name == "at" else prob[:, i % 2, 0:S]
                done(activate(prob[:, i % 2, 0:S], src, ACT.Exp, bias=negm[:, i % 2:i % 2 + 1],
                              accum_out=rsum[:, i % 2:i % 2 + 1]), exp_done)
                act.wait_ge(pt_mm, i + 1)
                if i >= 2:
                    act.wait_ge(pv_mm, i - 1)
                done(activate(probT[:, i % 2, 0:S], bank[6][:, 0:S], ACT.Copy), pt_ev)

            def turn(i, name, t):
                act.wait_ge(turn_mm, i + 1)
                tok = slice(t * P, (t + 1) * P)
                two = bank[3][:, 0:2 * P].rearrange("p (j c) -> p j c", j=2)
                if name == "qk":
                    done(activate(att[:, 0:2, tok], two, ACT.Copy, scale=HD ** -0.5))
                    ins = activate(att[:, 2, tok], bank[3][:, 2 * P:3 * P], ACT.Copy)
                elif name == "cy":
                    ins = activate(cvz[:, t, :], bank[3][:, 0:BW], ACT.Copy)
                elif name == "am":
                    q = bank[3][:, 0:P].rearrange("p (q r) -> p q r", q=4)
                    done(activate(am[:, t, :, :], q[:, 0:2, 0:HEADS], ACT.Copy))
                    ins = activate(em[:, t, :, :], q[:, 2:4, 0:HEADS], ACT.Exp, scale=-1.0)
                else:
                    n = {"na": 0, "ml": 1, "cv": 2, "at": 3}[name]
                    ins = activate(oT[:, 2 * n:2 * n + 2, tok], two, ACT.Copy, scale=0.5 if name == "cv" else 1.0)
                done(ins, turn_ev)

            def gates():
                act.wait_ge(lsig_min, 1)
                r = sum_rows[0:64, :]
                done(activate(r, top_rows[64:128, :], ACT.Abs))
                done(activate(r, r, ACT.Exp, scale=-1.0))
                done(activate(r, r, ACT.Ln, bias=1.0), lsig_ln)

            def ml(i, g, h):
                first, n = GROUPS[g]
                S = n * P
                if i == 0:
                    act.wait_ge(score_free, ATT_UNITS)
                else:
                    act.wait_ge(mlpv_mm, i)
                for d in range(2):
                    act.wait_ge(masked, 2 * i + d + 1)
                    for j in range(n):
                        a = am[:, first + j, d, h:h + 1]
                        lo, hi = ((j + 1) * P, S) if d == 0 else (0, j * P)
                        if hi > lo:
                            done(activate(mlw[:, d, j, lo:hi], bank[2][:, lo:hi], ACT.Exp, bias=a, scale=-1.0))
                        ins = activate(mlw[:, d, j, j * P:(j + 1) * P], dg[:, j * P:(j + 1) * P], ACT.Exp, bias=a,
                                       scale=-1.0)
                        done(ins, decay_done if j == n - 1 else None)

            def cnorm(i):
                act.wait_ge(cz_done, 1)
                done(activate(cvt, cvz, ACT.Tanh, scale=0.5), ctanh_done)

            for kind, i, key in steps:
                if kind == "gates":
                    gates()
                elif kind in ("proj", "attend", "turn", "ml", "cnorm"):
                    {"proj": proj, "attend": attend, "turn": turn, "ml": ml, "cnorm": cnorm}[kind](i, *key)

        def mix_vector(dve):
            done = Tally(dve, v_mix)
            h4 = lambda a: a.rearrange("p t (h d) -> p t h d", d=HD)
            row = lambda o, n: rows[:, o:o + n].unsqueeze(1).to_broadcast([P, T, n])

            def glu(i):
                dve.wait_ge(proj_ev, at[("proj", "cv", 7)] + 1)
                for lo, n, off in SEGS:
                    done(stt(cvx[:, :, PAD + off:PAD + off + n], cvag[:, 2:4, lo:lo + n], 1.0,
                             cvag[:, 0:2, lo:lo + n], ALU.add, ALU.mult))

            def conv(i):
                for k in range(TAPS * i // ATT_UNITS, TAPS * (i + 1) // ATT_UNITS):
                    for j in range(2):
                        w, y, src = pp[:, PP_CW + TAPS * j + k:PP_CW + TAPS * j + k + 1], cvy[:, j, :], cvx[
                            :, j, k:k + CONV_OUT]
                        last = conv_done if (k, j) == (TAPS - 1, 1) else None
                        if k == 0:
                            done(ts_(y, src, w, pp[:, PP_CB + j:PP_CB + j + 1], ALU.mult, ALU.add), last)
                        else:
                            done(stt(y, src, w, y, ALU.mult, ALU.add), last)

            def rope(i):
                dve.wait_ge(proj_ev, at[("proj", "at", T - 1)] + 1)
                qk = atr[:, :, 0:384]
                done(tt(rope_tmp, qk, qk, ALU.mult))
                done(reduce_(msq[:, 0:36].rearrange("p (t h) -> p t h", t=T), h4(rope_tmp), AX.X, ALU.add))
                done(ts_(msq[:, 0:36], msq[:, 0:36], 1.0 / HD, EPS, ALU.mult, ALU.add), mix_var)
                dve.wait_ge(mix_rs, 1)
                r = rstd[:, 0:36].rearrange("p (t h) -> p t h", t=T).unsqueeze(3).to_broadcast([P, T, 6, HD])
                done(tt(h4(qk), h4(qk), r, ALU.mult))
                done(tt(qk, qk, row(R_ATT, 384), ALU.mult))
                for a in range(4):
                    o, other = 16 * a, 16 * (a ^ 1)
                    s = sin[:, :, o:o + 16].unsqueeze(2).to_broadcast([P, T, 6, 16])
                    done(tt(h4(rope_tmp)[:, :, :, o:o + 16], h4(qk)[:, :, :, other:other + 16], s, ALU.mult))
                done(tt(h4(qk), h4(qk), cos.unsqueeze(2).to_broadcast([P, T, 6, HD]), ALU.mult))
                done(tt(qk, qk, rope_tmp, ALU.add), rope_done)

            def maximum(i, name, tile, h):
                S = GROUPS[tile_group(tile)][1] * P
                s, m = bank[4 + i % 2][:, 0:S], negm[:, i % 2:i % 2 + 1]
                dve.wait_ge(score_mm, i + 1)
                if i >= 2:
                    dve.wait_ge(exp_done, i - 1)
                if name == "na":
                    dve.wait_ge(pt_mm, i - 1)
                    r = tile - GROUPS[tile_group(tile)][0]
                    grid = lambda a: a.rearrange("p (r c) -> p r c", c=GRID)
                    done(tt(grid(prob[:, i % 2, 0:S]), grid(s), bias_tab[:, h, 7 - 2 * r:7 - 2 * r + S // GRID, :],
                            ALU.add), score_free)
                    s = prob[:, i % 2, 0:S]
                done(reduce_(m, s, AX.X, ALU.max, negate=True), max_done)

            def attend(i, name, tile, h):
                if i == 0 or attends[i - 1][0] != name:
                    maximum(i, name, tile, h)
                if i + 1 < len(attends) and attends[i + 1][0] == name:
                    maximum(i + 1, *attends[i + 1])
                dve.wait_ge(exp_done, i + 1)
                done(nc.vector.reciprocal(rrec, rsum[:, i % 2:i % 2 + 1]))
                dve.wait_ge(pv_mm, i + 1)
                if h == 0 and (name, tile) not in (("at", 0), ("at", 1)):
                    prev = (name, tile - 2) if tile >= 2 else ("at", tile + 4)
                    dve.wait_ge(turn_mm, at[("turn", *prev)] + 1)
                done(ts_(outb[:, tile % 2, HD * h:HD * h + HD], bank[7][:, HD * h:HD * h + HD], rrec, None, ALU.mult),
                     head_done)

            def cnorm(i):
                dve.wait_ge(turn_ev, at[("turn", "cy", T - 1)] + 1)
                z, per_token = cvz, lambda a: a.unsqueeze(2).to_broadcast([P, T, BW])
                done(reduce_(lmean, z, AX.X, ALU.add))
                done(ts_(lmean, lmean, 1.0 / BW, None, ALU.mult))
                done(tt(z, z, per_token(lmean), ALU.subtract))
                done(tt(cvt, z, z, ALU.mult))
                done(reduce_(msq[:, 0:T], cvt, AX.X, ALU.add))
                done(ts_(msq[:, 0:T], msq[:, 0:T], 1.0 / BW, EPS, ALU.mult, ALU.add), mix_var)
                dve.wait_ge(mix_rs, 2)
                done(tt(z, z, per_token(rstd[:, 0:T]), ALU.mult))
                done(tt(z, z, row(R_CG, BW), ALU.mult))
                done(tt(z, z, row(R_CB, BW), ALU.add), cz_done)
                dve.wait_ge(ctanh_done, 1)
                done(stt(z, cvt, 1.0, z, ALU.add, ALU.mult), cn_done)

            def bias(i):
                dve.wait_ge(bias_in_sem, 16)
                t = wide[:, :].rearrange("p (a c) -> p a c", c=GRID)
                done(tt(t, t, win.unsqueeze(1).to_broadcast([P, CW // GRID, GRID]), ALU.add), bias_done)

            def gates():
                fw, bw = slice(0, 32), slice(32, 64)
                dve.wait_ge(proj_ev, at[("proj", "mg", 1)] + 1)
                done(ts_(am_rows[0:64, :], top_rows[64:128, :], 0.0, None, ALU.min), lsig_min)
                dve.wait_ge(lsig_ln, 1)
                done(tt(am_rows[0:64, :], am_rows[0:64, :], sum_rows[0:64, :], ALU.subtract))
                for g, (first, n) in enumerate(GROUPS):
                    lo, S = first * P, n * P
                    seg = slice(lo, lo + S)
                    done(scan(sum_rows[0:64, seg], ones[0:64, 0:S], am_rows[0:64, seg], 0.0, ALU.mult, ALU.add))
                    done(nc.vector.tensor_copy(dg[bw, 1:S], sum_rows[bw, lo:lo + S - 1]))
                    done(nc.vector.memset(dg[bw, 0:1], 0.0))
                    done(tt(am_rows[fw, seg], top_rows[fw, seg], sum_rows[fw, seg], ALU.subtract))
                    done(tt(am_rows[bw, seg], top_rows[bw, seg], dg[bw, 0:S], ALU.add))
                    done(scan(top_rows[fw, seg], am_rows[fw, seg], am_rows[fw, seg], NEG, ALU.max, ALU.max))
                    back = am_rows[bw, seg][:, ::-1]
                    done(scan(top_rows[bw, seg][:, ::-1], back, back, NEG, ALU.max, ALU.max))
                    done(tt(am_rows[64:96, seg], top_rows[fw, seg], sum_rows[fw, seg], ALU.add))
                    done(tt(am_rows[96:128, seg], top_rows[bw, seg], dg[bw, 0:S], ALU.subtract),
                         rows_done if g == 1 else None)

            s_next = units_of["score"]

            def ml(i, g, h):
                nonlocal s_next
                first, n = GROUPS[g]
                S = n * P
                for d in range(2):
                    dve.wait_ge(decay_mm, 2 * i + d + 1)
                    if i or d:
                        dve.wait_ge(decay_done, 2 * i + d)
                    blocks = lambda a: a.rearrange("p (j c) -> p j c", c=P)
                    done(tt(blocks(dg[:, 0:S]), blocks(bank[2][:, 0:S]),
                            tri[:, d, :].unsqueeze(1).to_broadcast([P, n, P]), ALU.add), masked)
                dve.wait_ge(decay_done, 2 * i + 2)
                for j in range(n):
                    dve.wait_ge(score_mm, s_next + 1)
                    b = bank[4 + s_next % 2]
                    s_next += 1
                    w0, w1 = mlw[:, 0, j, j * P:S], mlw[:, 1, j, 0:(j + 1) * P]
                    done(tt(w0, b[:, j * P:S], w0, ALU.mult))
                    done(tt(w1, b[:, 0:(j + 1) * P], w1, ALU.mult), score_free)
                dve.wait_ge(turn_ev, at[("turn", "am", T - 1)] + 1)
                dve.wait_ge(mlpv_mm, i + 1)
                num = [bank[6 + d][:, 0:65 * n].rearrange("p (t c) -> p t c", c=65) for d in range(2)]
                for d in range(2):
                    done(nc.vector.tensor_copy(den[:, d, 0:n], num[d][:, :, HD]))
                done(stt(den2[:, :, 0:n], den[:, :, 0:n], -1.0, den[:, :, 0:n], ALU.mult, ALU.max))
                e = em[:, first:first + n, :, h].rearrange("p t d -> p d t")
                done(tt(den2[:, :, 0:n], den2[:, :, 0:n], e, ALU.max))
                done(nc.vector.reciprocal(den[:, :, 0:n], den2[:, :, 0:n]))
                o, tmp = hm[:, first:first + n, HD * h:HD * h + HD], dg[:, 0:HD * n].rearrange("p (t c) -> p t c", c=HD)
                r = [den[:, d, 0:n].unsqueeze(2).to_broadcast([P, n, HD]) for d in range(2)]
                done(tt(o, num[0][:, :, 0:HD], r[0], ALU.mult))
                done(tt(tmp, num[1][:, :, 0:HD], r[1], ALU.mult))
                done(tt(o, o, tmp, ALU.add), mlh_done)

            def mnorm(i):
                sq = wide[:, 0:1536].rearrange("p (t c) -> p t c", t=T)
                done(tt(sq, hm, hm, ALU.mult))
                done(reduce_(msq[:, 0:24].rearrange("p (t h) -> p t h", t=T), h4(sq), AX.X, ALU.add))
                done(ts_(msq[:, 0:24], msq[:, 0:24], 1.0 / HD, EPS, ALU.mult, ALU.add), mix_var)
                dve.wait_ge(mix_rs, 3)
                done(ts_(rstd[:, 0:24], rstd[:, 0:24], 0.5, None, ALU.mult))
                r = rstd[:, 0:24].rearrange("p (t h) -> p t h", t=T).unsqueeze(3).to_broadcast([P, T, HEADS, HD])
                done(tt(h4(hm), h4(hm), r, ALU.mult))
                done(tt(hm, hm, row(R_ML, BW), ALU.mult))
                done(stt(hm, mlo, 1.0, hm, ALU.add, ALU.mult), mn_done)

            for kind, i, key in steps:
                if kind == "gates":
                    gates()
                elif kind in ("glu", "rope", "conv", "cnorm", "bias", "attend", "ml", "mnorm"):
                    {"glu": glu, "rope": rope, "conv": conv, "cnorm": cnorm, "bias": bias, "attend": attend,
                     "ml": ml, "mnorm": mnorm}[kind](i, *key)

        def mix(layer):
            with nc.Block() as block:
                @block.sync
                def _(sp):
                    for c in range(MIX_CHUNKS + 2):
                        if c >= 2:
                            sp.wait_ge(proj_mm, last_proj[c - 2] + 1)
                        load_chunk(sp, layer, c)
                        if c == 1:
                            sp.dma_start(wide[:, :], bias_in[bass.ds(layer, 1)].rearrange("a p n -> (a p) n")
                                         ).then_inc(bias_in_sem, 16)

                @block.gpsimd
                def _(pool):
                    for r, n in enumerate([36, T, 24]):
                        pool.wait_ge(mix_var, r + 1)
                        nc.gpsimd.tensor_tensor(rstd[:, 0:n], msq[:, 0:n], nhalf[:, 0:n], ALU.pow).then_inc(mix_rs, 1)

                block.tensor(mix_tensor)
                block.scalar(mix_scalar)
                block.vector(mix_vector)

        def merge(layer):
            units = [(m, n, hf) for m in range(KD) for n in range(NBR) for hf in range(2)]
            half = [slice(0, HALF), slice(HALF, TOK)]
            wb_sb = [wide[:, :].rearrange("p (n k c) -> p n k c", n=NBR, k=2),
                     reg_a[:, 0:CW].rearrange("p (n k c) -> p n k c", n=NBR, k=2)]
            with nc.Block() as block:
                @block.sync
                def _(sp):
                    for c in range(2):
                        sp.dma_start((wide[:, :], reg_a[:, 0:CW])[c], wb[bass.ds(layer * 2 + c, 1)]
                                     .rearrange("a p n -> (a p) n")).then_inc(wb_in, 16)
                    sp.dma_start(wr_sb[:, :, :].rearrange("p k n -> p (k n)"),
                                 wr[bass.ds(layer, 1)].rearrange("a p n -> (a p) n")).then_inc(wr_in, 16)
                    for c in range(MIX_CHUNKS + 2, CHUNKS):
                        sp.wait_ge(gate_mm, 8 * (c - MIX_CHUNKS - 1))
                        load_chunk(sp, layer, c)

                @block.tensor
                def _(pe):
                    pe.wait_ge(wb_in, 32)
                    for q, (m, n, hf) in enumerate(units):
                        c = MIX_CHUNKS + m
                        w = ring[:, c % 2, :].rearrange("p (k n) -> p k n", k=KD)
                        wait_chunk(pe, c)
                        if q >= 4:
                            pe.wait_ge(tanh_done, q - 3)
                        for k in range(KD):
                            mm = nc.tensor.matmul(bank[q % 4][:, 0:HALF], w[:, k, n * P:(n + 1) * P], hT[:, k, half[hf]],
                                                  start=(k == 0), stop=(k == KD - 1))
                        mm.then_inc(gate_mm, 1)
                        if q >= 4:
                            pe.wait_ge(gated, q - 3)
                        for k in range(2):
                            mm = nc.tensor.matmul(bank[4 + q % 4][:, 0:HALF],
                                                  wb_sb[m // 4][:, n, k, (m % 4) * P:(m % 4 + 1) * P],
                                                  oT[:, 2 * n + k, half[hf]], start=(k == 0), stop=(k == 1))
                        mm.then_inc(branch_mm, 1)
                    pe.wait_ge(merged, 2 * KD)
                    pe.wait_ge(tanh_done, len(units))
                    for o in range(2 * T):
                        c, t = CHUNKS - 2 + o // T, o % T
                        w = ring[:, c % 2, :].rearrange("p (k n) -> p k n", k=KD)
                        wait_chunk(pe, c)
                        if o >= 4:
                            pe.wait_ge(out_ev, o - 3)
                        for k in range(KD):
                            mm = nc.tensor.matmul(bank[o % 4][:, :], mT[:, k, t * P:(t + 1) * P], w[:, k, :],
                                                  start=(k == 0), stop=(k == KD - 1))
                        mm.then_inc(out_mm, 1)

                @block.scalar
                def _(act):
                    act.wait_ge(bgh_done, 1)
                    for q, (m, n, hf) in enumerate(units):
                        act.wait_ge(gate_mm, q + 1)
                        if q >= 4:
                            act.wait_ge(gated, q - 3)
                        activate(tanh_buf[q % 4], bank[q % 4][:, 0:HALF], ACT.Tanh, scale=0.5,
                                 bias=bg_half[:, NBR * m + n:NBR * m + n + 1]).then_inc(tanh_done, 1)

                @block.vector
                def _(dve):
                    done = Tally(dve, v_merge)
                    done(ts_(bg_half, pp[:, PP_BG:PP_BG + 32], 0.5, None, ALU.mult), bgh_done)
                    for q, (m, n, hf) in enumerate(units):
                        dve.wait_ge(tanh_done, q + 1)
                        dve.wait_ge(branch_mm, q + 1)
                        to, tmp = mT[:, m, half[hf]], dg[:, 0:HALF]
                        done(stt(tmp if n else to, tanh_buf[q % 4], 1.0, bank[4 + q % 4][:, 0:HALF], ALU.add, ALU.mult),
                             gated)
                        if n:
                            done(tt(to, to, tmp, ALU.add), merged if n == NBR - 1 else None)
                    for o in range(2 * T):
                        c, t = o // T, o % T
                        dve.wait_ge(out_mm, o + 1)
                        xs = x[:, t, c * 512:(c + 1) * 512]
                        done(stt(xs, bank[o % 4][:, :], 0.5, xs, ALU.mult, ALU.add), out_ev)

        def experts(layer):
            def wexp(s):
                w13 = slot_w[s][:, 0:KD * 2 * DE].rearrange("p (k n) -> p k n", k=KD)
                w2 = slot_w[s][:, KD * 2 * DE:EW].rearrange("p (k n) -> p k n", k=2)
                return w13, w2

            lg = rt[:, 0:120].rearrange("p (t e) -> p t e", t=T)
            g6 = lambda a: a.unsqueeze(2).to_broadcast([P, T, NG])
            col = lambda o: rt[:, o:o + T]
            four = lambda o: rt[:, o:o + 24].rearrange("p (t g) -> p t g", t=T)
            gl, el = lg[:, :, 0:NG], lg[:, :, NG:NG + NE]
            gmax, gsum, top1, top2, w1, w2, ex = (col(120 + 6 * i) for i in range(7))
            dexp = rt[:, 168:198].rearrange("p (t c) -> p t c", t=T)
            group1, first1, first2, ein, masked_e, cand, c4 = (four(200 + 24 * i) for i in range(7))
            prod = rt[:, 400:496].rearrange("p (t g j) -> p t g j", t=T, g=NG)
            nbody = 2 * T
            hidb = [prob[:, 0, 0:DE], prob[:, 1, 0:DE]]
            thb = [prob[:, 0, DE:2 * DE], prob[:, 1, DE:2 * DE]]
            hidT = [probT[:, i, 0:DE].rearrange("p (k c) -> p k c", k=2) for i in range(2)]

            with nc.Block() as block:
                @block.sync
                def _(sp):
                    with sp.Fori(1, NE // 2) as e2:
                        for s in range(2):
                            sp.wait_ge(down_mm, e2 * nbody + s * T - T)
                            sp.dma_start(slot_w[s], we[bass.ds(layer * NE + e2 * 2 + s, 1)]
                                         .rearrange("a p n -> (a p) n")).then_inc(expert_in[s], 16)

                @block.tensor
                def _(pe):
                    pe.wait_ge(wr_in, 16)
                    for t in range(T):
                        for k in range(KD):
                            mm = nc.tensor.matmul(bank[0][:, t * 20:(t + 1) * 20], hT[:, k, t * P:(t + 1) * P],
                                                  wr_sb[:, k, :], start=(k == 0), stop=(k == KD - 1))
                    mm.then_inc(route_mm, 1)
                    pe.wait_ge(comb_done, 1)

                    def up(e2, v):
                        s, t = v // T, v % T
                        if t == 0:
                            pe.wait_ge(expert_in[s], 16 * e2 + 16)
                        pe.wait_ge(hid_done, e2 * nbody + v + 1)
                        for k in range(KD):
                            mm = nc.tensor.matmul(bank[v % 2][:, :], hT[:, k, t * P:(t + 1) * P], wexp(s)[0][:, k, :],
                                                  start=(k == 0), stop=(k == KD - 1))
                        mm.then_inc(up_mm, 1)

                    def down(e2, v):
                        s = v // T
                        pe.wait_ge(hid_done, e2 * nbody + v + 3)
                        pe.wait_ge(hid_ev, e2 * nbody + v + 1)
                        for k in range(2):
                            mm = nc.tensor.transpose(bank[2 + v % 2][:, k * P:(k + 1) * P],
                                                     hidb[v % 2][:, k * P:(k + 1) * P], ident)
                        mm.then_inc(hid_mm, 1)
                        pe.wait_ge(hid_ev, e2 * nbody + v + 3)
                        pe.wait_ge(y_ev, e2 * nbody + v + 1)
                        for c in range(2):
                            for k in range(2):
                                mm = nc.tensor.matmul(bank[4 + 2 * (v % 2) + c][:, :], hidT[v % 2][:, k, :],
                                                      wexp(s)[1][:, k, c * 512:(c + 1) * 512],
                                                      start=(k == 0), stop=(k == 1))
                        mm.then_inc(down_mm, 1)

                    with pe.Fori(0, NE // 2) as e2:
                        up(e2, 0)
                        for v in range(nbody):
                            if v + 1 < nbody:
                                up(e2, v + 1)
                            down(e2, v)

                @block.scalar
                def _(act):
                    act.wait_ge(route_diff, 1)
                    activate(dexp[:, :, 0:NG], dexp[:, :, 0:NG], ACT.Exp).then_inc(route_exp, 1)
                    act.wait_ge(route_diff, 2)
                    activate(ex, ex, ACT.Exp).then_inc(route_exp, 1)
                    act.sem_inc(hid_ev, 2)
                    with act.Fori(0, NE // 2) as e2:
                        for v in range(nbody):
                            act.wait_ge(up_mm, e2 * nbody + v + 1)
                            act.wait_ge(hid_done, e2 * nbody + v + 1)
                            activate(thb[v % 2], bank[v % 2][:, 0:DE], ACT.Tanh, scale=0.5).then_inc(th_done, 1)
                            act.wait_ge(hid_mm, e2 * nbody + v + 1)
                            activate(hidT[v % 2], bank[2 + v % 2][:, 0:DE].rearrange("p (k c) -> p k c", k=2),
                                     ACT.Copy).then_inc(hid_ev, 1)

                @block.vector
                def _(dve):
                    done = Tally(dve, v_route)

                    def first_of(src, best, to):
                        done(tt(cand, src, g6(best), ALU.is_equal))
                        done(ts_(cand, cand, -16.0, 16.0, ALU.mult, ALU.add))
                        done(tt(cand, cand, iota4.unsqueeze(1).to_broadcast([P, T, NG]), ALU.add))
                        done(reduce_(ex, cand, AX.X, ALU.min))
                        done(tt(to, cand, g6(ex), ALU.is_equal))

                    dve.wait_ge(route_mm, 1)
                    done(tt(lg, bank[0][:, 0:120].rearrange("p (t e) -> p t e", t=T),
                            rows[:, R_MOE:R_MOE + 20].unsqueeze(1).to_broadcast([P, T, 20]), ALU.add))
                    done(reduce_(gmax, gl, AX.X, ALU.max))
                    done(tt(dexp[:, :, 0:NG], gl, g6(gmax), ALU.subtract), route_diff)
                    first_of(gl, gmax, group1)
                    by_group = group1.unsqueeze(3).to_broadcast([P, T, NG, 4])
                    done(tt(prod, el.rearrange("p t (g j) -> p t g j", g=NG), by_group, ALU.mult))
                    done(reduce_(ein, prod.rearrange("p t g j -> p t j g"), AX.X, ALU.add))
                    done(reduce_(top1, ein, AX.X, ALU.max))
                    first_of(ein, top1, first1)
                    done(stt(masked_e, first1, NEG, ein, ALU.mult, ALU.add))
                    done(reduce_(top2, masked_e, AX.X, ALU.max))
                    first_of(masked_e, top2, first2)
                    dve.wait_ge(route_exp, 1)
                    done(reduce_(gsum, dexp[:, :, 0:NG], AX.X, ALU.add))
                    done(tt(ex, top2, top1, ALU.subtract), route_diff)
                    dve.wait_ge(route_exp, 2)
                    done(ts_(w1, ex, 1.0, 2.0, ALU.add, ALU.mult))
                    done(tt(w1, w1, gsum, ALU.mult))
                    done(nc.vector.reciprocal(w1, w1))
                    done(tt(w2, w1, ex, ALU.mult))
                    done(tt(first1, first1, g6(w1), ALU.mult))
                    done(tt(first2, first2, g6(w2), ALU.mult))
                    done(tt(c4, first1, first2, ALU.add))
                    done(tt(comb.rearrange("p t (g j) -> p t g j", g=NG), by_group,
                            c4.unsqueeze(2).to_broadcast([P, T, NG, 4]), ALU.mult), comb_done)

                    dve.sem_inc(hid_done, 2)
                    dve.sem_inc(y_ev, 2)
                    with dve.Fori(0, NE // 2) as e2:
                        for v in range(nbody):
                            s, t = v // T, v % T
                            dve.wait_ge(th_done, e2 * nbody + v + 1)
                            stt(thb[v % 2], thb[v % 2], 1.0, bank[v % 2][:, 0:DE], ALU.add, ALU.mult).then_inc(v_exp, 1)
                            dve.wait_ge(v_exp, e2 * nbody + v + 1)
                            stt(hidb[v % 2], bank[v % 2][:, DE:2 * DE], comb[:, t, bass.ds(e2 * 2 + s, 1)], thb[v % 2],
                                ALU.mult, ALU.mult).then_inc(hid_done, 1)
                            dve.wait_ge(down_mm, e2 * nbody + v + 1)
                            for c in range(2):
                                xs = x[:, t, c * 512:(c + 1) * 512]
                                ins = tt(xs, bank[4 + 2 * (v % 2) + c][:, :], xs, ALU.add)
                            ins.then_inc(y_ev, 1)

        def read_layer_params(layer):
            def read(sp):
                sp.dma_start(pp[:, :], pp_in[bass.ds(layer, 1)].rearrange("a p n -> (a p) n")).then_inc(params_in, 16)
                sp.dma_start(rows[:, :], rows_in[bass.ds(layer, 1), :].to_broadcast([P, R_N])).then_inc(params_in, 16)
            return read

        def read_first_experts(layer):
            def read(sp):
                for s in range(2):
                    sp.dma_start(slot_w[s], we[bass.ds(layer * NE + s, 1)].rearrange("a p n -> (a p) n")
                                 ).then_inc(expert_in[s], 16)
            return read

        with nc.Fori(0, L) as layer:
            normalised("norm1", read_layer_params(layer), PP_GMIX, sem)
            mix(layer)
            merge(layer)
            normalised("norm2", read_first_experts(layer), PP_GFFN, sem)
            experts(layer)
            first, last = min(layer_sems), max(layer_sems)
            assert last - first + 1 == len(layer_sems)
            nc.gpsimd.sem_clear(range(first, last + 1))
            nc.all_engine_barrier()
        normalised("final", lambda sp: sp.dma_start(reg_a[:, 3 * D:4 * D], fin_in[0:1, :].to_broadcast([P, D])
                                                    ).then_inc(inputs_in, 16), None, once)


def constants():
    c = np.zeros((P, C_N), np.float32)
    c[:, C_ID:C_ID + P] = np.eye(P)
    p = np.arange(P)
    inv = np.float32(10000.0) ** (-np.arange(0, HD // 2, 2, dtype=np.float32) / np.float32(HD // 2))
    for tile in range(T):
        tok = (tile - GROUPS[tile_group(tile)][0]) * P + p
        pos = np.stack([tok // GRID, tok % GRID], -1).astype(np.float32)
        ang = (pos[:, :, None] * inv.astype(np.float32)).astype(np.float32)
        cos, sin = np.cos(ang), np.sin(ang)
        c[:, C_COS + HD * tile:C_COS + HD * (tile + 1)] = np.concatenate([cos, cos], -1).reshape(P, HD)
        c[:, C_SIN + HD * tile:C_SIN + HD * (tile + 1)] = np.concatenate([-sin, sin], -1).reshape(P, HD)
    q, k = (p % GRID)[:, None], np.arange(GRID)[None]
    start = np.clip(q - 8, 0, GRID - 16)
    c[:, C_WIN:C_WIN + GRID] = np.where((k >= start) & (k < start + 16), 0.0, NEG)
    s, t = p[:, None], p[None]
    c[:, C_TRI:C_TRI + P] = np.where(s > t, -NEG, 0.0)
    c[:, C_TRI + P:C_TRI + 2 * P] = np.where(s < t, -NEG, 0.0)
    for j in range(8):
        c[32 * (j // 4) + j % 4, C_SEL + j * P:C_SEL + (j + 1) * P] = 1.0
    c[:, C_IOTA:C_IOTA + 4] = np.arange(4)
    return c


def laid_out(a):
    kp = lambda w: np.moveaxis(w.reshape(w.shape[0], KD, P, -1), 1, 2).reshape(w.shape[0], P, -1)
    w = a["w_in"]
    na, ml, gt, cv, at = 0, 768, 768 + 1024, 768 + 1040, 768 + 1040 + 512
    last = np.zeros((L, D, 512), w.dtype)
    last[:, :, 0:BW] = w[:, :, ml + 768:ml + 1024]
    pp = np.zeros((L, P, PP_N), w.dtype)
    for row, src in ((0, 0), (64, 4), (32, 8), (96, 12)):
        last[:, :, BW + row:BW + row + 4] = w[:, :, gt + src:gt + src + 4]
        pp[:, row:row + 4, PP_GB] = a["ml_gate_b"].reshape(L, 16)[:, src:src + 4]
    gate = a["w_gate"].reshape(L, D, NBR, KD, P)
    att_q = w[:, :, at:at + BW].reshape(L, D, 2, 2, HD).transpose(0, 1, 3, 2, 4).reshape(L, D, BW)
    chunks = [w[:, :, cv:cv + 512], np.concatenate([att_q, w[:, :, at + BW:at + 512]], 2),
              w[:, :, na:na + 512],
              np.concatenate([w[:, :, na + 512:na + 768], w[:, :, ml + 512:ml + 768]], 2), w[:, :, ml:ml + 512], last]
    chunks += [gate[:, :, :, m].reshape(L, D, 512) for m in range(KD)]
    chunks += [a["w_out"][:, :, c * 512:(c + 1) * 512] for c in range(2)]
    assert len(chunks) == CHUNKS
    wd = np.stack([kp(c) for c in chunks], 1).reshape(L * CHUNKS, P, CW)
    wb = a["w_branch"].reshape(L, NBR, 2, P, 2, 512).transpose(0, 4, 3, 1, 2, 5).reshape(L * 2, P, CW)
    w13 = np.concatenate([a["moe_w1"], a["moe_w3"]], 3).reshape(L * NE, D, 2 * DE)
    w2 = a["moe_w2"].reshape(L * NE, 2, P, D).transpose(0, 2, 1, 3).reshape(L * NE, P, 2 * D)
    we = np.concatenate([kp(w13), w2], 2)
    wr = kp(np.concatenate([a["moe_w_group"], a["moe_w_expert"].reshape(L, D, NE)], 2))
    turned = lambda v, n: v.reshape(L, n, P).transpose(0, 2, 1)
    pp[:, :, PP_GMIX:PP_GMIX + KD] = turned(a["norm_mix_g"], KD)
    pp[:, :, PP_GFFN:PP_GFFN + KD] = turned(a["norm_ffn_g"], KD)
    pp[:, :, PP_CW:PP_CW + 2 * TAPS] = a["conv_dw_w"].reshape(L, TAPS, 2, P).transpose(0, 3, 2, 1).reshape(L, P, -1)
    pp[:, :, PP_CB:PP_CB + 2] = turned(a["conv_dw_b"], 2)
    pp[:, :, PP_BG:PP_BG + 32] = a["b_gate"].reshape(L, NBR, KD, P).transpose(0, 3, 2, 1).reshape(L, P, 32)
    rows = np.concatenate([np.tile(a["att_q_norm_g"], (1, HEADS)), np.tile(a["att_k_norm_g"], (1, 2)), a["ml_norm_g"],
                           a["conv_norm_g"], a["conv_norm_b"], a["moe_b_group"],
                           a["moe_b_expert"].reshape(L, NE)], 1)
    c = np.arange(GRID)
    off = np.clip(c[None, :] - c[:, None] + 15, 0, 30)
    side = np.arange(2)[:, None]
    r = np.clip(np.arange(16)[None] - side, 0, 14)
    bias = a["na_rpb"][:, :, r[:, :, None, None], off[None, None]]
    bias = bias.transpose(0, 2, 4, 1, 3, 5).reshape(L, P, CW)
    return dict(x_prompt=a["x_prompt"], x_sample=a["x_sample"], wd=wd, wb=wb, we=we, wr=wr, pp=pp, rows=rows,
                fin=a["final_norm_g"].reshape(1, D), bias=bias, consts=constants())


def kernel(**inputs):
    import concourse.bacc as bacc
    from concourse.bass_utils import run_bass_kernel_spmd

    nc = bacc.Bacc("TRN2", target_bir_lowering=False, num_devices=1)
    arrays, args = {}, []
    for name, a in laid_out({k: np.asarray(v) for k, v in inputs.items()}).items():
        a = np.ascontiguousarray(a)
        arrays[f"in_{name}"] = a
        args.append(nc.dram_tensor(f"in_{name}", a.shape, mybir.dt.from_np(a.dtype), kind="ExternalInput").ap())
    outs = {"y_prompt": (1, 256, D), "y_sample": (1, 512, D)}
    for name, shape in outs.items():
        args.append(nc.dram_tensor(name, shape, F32, kind="ExternalOutput").ap())
    program(nc, *args)
    r = run_bass_kernel_spmd(nc, [arrays], core_ids=[0])
    return tuple(r.results[0][name] for name in outs)
```

```python
from contextlib import ExitStack

import numpy as np

import concourse.bass as bass
from concourse import mybir

F32 = mybir.dt.float32
ALU = mybir.AluOpType
ACT = mybir.ActivationFunctionType
AX = mybir.AxisListType

P = 128
D = 1024
KD = D // P
L = 2
GROUPS = [(0, 2), (2, 4)]
T = sum(n for _, n in GROUPS)
TOK = T * P
HALF = TOK // 2
GRID = 64
HD = 64
BW = 256
HEADS = 4
TAPS = 31
PAD = TAPS // 2
NBR = 4
NG = 4
NE = 16
DE = 256
TOP = 2
SPARE = 12
assert TOP * TOK // (P + 1) <= SPARE
BLOCKS = NE + SPARE
EPS = 1e-6
NEG = -1e30
CHUNKS = 16
MIX_CHUNKS = 14
CW = KD * 512
EW = KD * 2 * DE + 2 * D
SEGS = [(0, 256, 0), (256, 512, 256 + PAD)]
CONV_OUT = TOK + PAD
CONV_IN = TOK + 3 * PAD
ATT_UNITS = T * HEADS

PP_GMIX, PP_GFFN, PP_CW, PP_CB, PP_GB, PP_BG = 0, 8, 16, 78, 80, 81
PP_N = 113
R_ATT, R_ML, R_CG, R_CB, R_MOE = 0, 384, 640, 896, 1152
R_N = 1172
C_ID, C_COS, C_SIN, C_WIN, C_TRI, C_IOTA, C_E128, C_BEFORE = 0, 128, 512, 896, 960, 1216, 1228, 1244
C_N = 1372


class Tally:

    def __init__(self, eng, chain):
        self.eng, self.chain, self.n = eng, chain, {}

    def __call__(self, ins, sem=None):
        sem = self.chain if sem is None else sem
        ins.then_inc(sem, 1)
        self.n[sem.num] = self.n.get(sem.num, 0) + 1
        self.eng.wait_ge(sem, self.n[sem.num])


def tile_group(tile):
    return 0 if tile < GROUPS[0][1] else 1


PROJ_UNITS = {"cv": 8, "at": 6, "na": 8, "nv": 6, "ml": 8, "mo": 6, "mg": 2}
CHUNK_NAMES = ["cv", "at", "gate0", "gate1", "gate2", "ml", "mo", "na", "nv", "gate3", "gate4", "gate5", "gate6",
               "gate7", "out0", "out1"]
GATE_UNITS = KD * NBR * 2


def chunk_of(name, u):
    return CHUNK_NAMES.index("mo" if name == "mg" else f"gate{u // (NBR * 2)}" if name == "gate" else name)


def schedule():
    steps, count, at = [], {}, {}

    def add(kind, *key):
        i = count.get(kind, 0)
        count[kind] = i + 1
        at[(kind, *key)] = i
        steps.append((kind, i, key))

    def proj(name):
        for u in range(PROJ_UNITS[name]):
            add("proj", name, u)

    gates_left = iter(range(GATE_UNITS))

    def gate():
        add("proj", "gate", next(gates_left))

    def attention(name, extra=None):
        units = [(name, tile, h) for tile in range(T) for h in range(HEADS)]
        add("score", *units[0])
        add("exp", *units[0])
        for i, u in enumerate(units):
            if i + 1 < len(units):
                add("score", *units[i + 1])
            if extra:
                add(extra)
            add("ptrans", *u)
            if i + 1 < len(units):
                add("exp", *units[i + 1])
            gate()
            add("attend", *u)
            if u[2] == HEADS - 1:
                add("turn", name, u[1])

    def turns(name):
        for t in range(T):
            add("turn", name, t)

    proj("cv")
    proj("at")
    add("glu")
    add("rope")
    turns("qk")
    attention("at", "conv")
    turns("cy")
    add("cnorm")
    for name in ("ml", "mo", "mg"):
        proj(name)
    add("gates")
    turns("cv")
    add("bias")
    for name in ("na", "nv"):
        proj(name)
    turns("am")
    attention("na")
    for h in range(HEADS):
        for g in range(len(GROUPS)):
            add("decay", g, h, 0)
            gate()
            add("decay", g, h, 1)
            gate()
            add("ml", g, h)
    add("mnorm")
    turns("ml")
    assert next(gates_left, None) is None
    return steps, at


def program(nc, x_prompt, x_sample, wd, wb, we, wr, pp_in, rows_in, fin_in, bias_in, ffn_in, consts_in, gate_dram, blocks, y_prompt, y_sample):
    steps, at = schedule()
    units_of = {}
    for kind, i, key in steps:
        units_of[kind] = i + 1
    last_proj = {}
    for kind, i, key in steps:
        if kind == "proj":
            last_proj[chunk_of(*key)] = i
    tt, ts_, stt = nc.vector.tensor_tensor, nc.vector.tensor_scalar, nc.vector.scalar_tensor_tensor
    reduce_, scan, activate = nc.vector.tensor_reduce, nc.vector.tensor_tensor_scan, nc.scalar.activation

    ctx = ExitStack()
    with ctx:
        def sb(name, shape):
            return ctx.enter_context(nc.sbuf_tensor(name, shape, F32))

        def once(name):
            return ctx.enter_context(nc.semaphore(name))

        layer_sems = []

        def sem(name):
            s = ctx.enter_context(nc.semaphore(name))
            layer_sems.append(s.num)
            return s

        x = sb("x", [P, T, D])
        hT = sb("hT", [P, KD, TOK])
        ring = sb("ring", [P, 2, CW])
        wide = sb("wide", [P, CW])
        reg_a = sb("reg_a", [P, 4608])
        reg_b = sb("reg_b", [P, 6200])
        oT = sb("oT", [P, 8, TOK])
        cvx = sb("cvx", [P, 2, CONV_IN])
        consts = sb("consts", [P, C_N])
        rows = sb("rows", [P, R_N])
        pp = sb("pp", [P, PP_N])
        prob = sb("prob", [P, 2, 512])
        probT = sb("probT", [P, 2, 512])
        outb = sb("outb", [P, 2, BW])
        am_rows = sb("am_rows", [P, TOK])
        dg = sb("dg", [P, 512])
        ones = sb("ones", [P, 4])
        gbuf = sb("gbuf", [P, 2, TOK])
        wr_sb = sb("wr_sb", [P, KD, NG + NE])
        small = sb("small", [P, 1024])
        slots = ctx.enter_context(nc.sbuf_tensor("slots", [P, T * TOP], mybir.dt.uint32))
        table = ctx.enter_context(nc.sbuf_tensor("table", [P, SPARE + 1], mybir.dt.int32))

        ident = consts[:, C_ID:C_ID + P]
        cos = consts[:, C_COS:C_COS + 384].rearrange("p (t d) -> p t d", t=T)
        sin = consts[:, C_SIN:C_SIN + 384].rearrange("p (t d) -> p t d", t=T)
        win = consts[:, C_WIN:C_WIN + GRID]
        tri = consts[:, C_TRI:C_TRI + 256].rearrange("p (d t) -> p d t", d=2)
        iota = consts[:, C_IOTA:C_IOTA + SPARE]
        e128 = consts[:, C_E128:C_E128 + NE]
        before = consts[:, C_BEFORE:C_BEFORE + P]

        cvag = reg_a[:, 0:4 * TOK].rearrange("p (j t) -> p j t", j=4)
        cvy = reg_a[:, 0:2 * CONV_OUT].rearrange("p (j t) -> p j t", j=2)
        cvz = reg_a[:, 3072:4608].rearrange("p (t c) -> p t c", t=T)
        naqk = reg_a[:, 0:4 * TOK].rearrange("p (j t) -> p j t", j=4)
        nav = reg_a[:, 3072:4608].rearrange("p (t c) -> p t c", t=T)
        hm = reg_a[:, 0:1536].rearrange("p (t c) -> p t c", t=T)
        atr = reg_b[:, 0:3072].rearrange("p (t c) -> p t c", t=T)
        att = reg_b[:, 3072:5376].rearrange("p (j t) -> p j t", j=3)
        mlqk = reg_b[:, 0:3072].rearrange("p (j t) -> p j t", j=4)
        mlv = reg_b[:, 3072:4632].rearrange("p (t h c) -> p t h c", t=T, h=HEADS)
        mlo = reg_b[:, 4632:6168].rearrange("p (t c) -> p t c", t=T)
        mT = reg_b[:, 0:KD * TOK].rearrange("p (k t) -> p k t", k=KD)
        rope_tmp = oT[:, 0:3, :].rearrange("p a (b c) -> p (a b) c", c=384)
        cvt = oT[:, 0:2, :].rearrange("p a (b c) -> p (a b) c", c=BW)
        top_rows, sum_rows = oT[:, 2, :], oT[:, 3, :]
        bias_tab = wide[:, :].rearrange("p (h r c) -> p h r c", h=HEADS, r=16)
        mlw = wide[:, :].rearrange("p (d j t) -> p d j t", d=2, j=4)
        h_rows = ring[:, :, :].rearrange("p a b -> p (a b)")[:, 0:T * D].rearrange("p (t d) -> p t d", t=T)
        slot_w = [oT[:, :, :].rearrange("p a b -> p (a b)")[:, 0:EW], reg_b[:, 0:EW]]

        msq, rstd, nhalf = small[:, 0:64], small[:, 64:128], small[:, 128:192]
        negm, rsum, rrec = small[:, 192:194], small[:, 194:196], small[:, 196:197]
        am = small[:, 200:248].rearrange("p (t d h) -> p t d h", t=T, d=2)
        em = small[:, 248:296].rearrange("p (t d h) -> p t d h", t=T, d=2)
        den = small[:, 296:304].rearrange("p (d t) -> p d t", d=2)
        den2 = small[:, 304:312].rearrange("p (d t) -> p d t", d=2)
        lmean = small[:, 312:318]
        bg_half = small[:, 320:352]
        rt = small[:, 352:1024]

        bank = [ctx.enter_context(nc.psum_tensor(f"bank{i}", [P, 512], F32)) for i in range(8)]

        rows_init = once("rows_init")
        scattered, gathered = once("scattered"), [once(f"gathered{t}") for t in range(T)]
        inputs_in, setup_done, stored = once("inputs_in"), once("setup_done"), [once("stored0"), once("stored1")]
        chunk_in = [sem("chunk_in0"), sem("chunk_in1")]
        params_in, bias_in_sem, wb_in, wr_in = sem("params_in"), sem("bias_in"), [sem("wb_in0"), sem("wb_in1")], sem("wr_in")
        expert_in = [sem("expert_in0"), sem("expert_in1")]
        proj_mm, turn_mm, score_mm, pt_mm, pv_mm = (sem("proj_mm"), sem("turn_mm"), sem("score_mm"), sem("pt_mm"),
                                                    sem("pv_mm"))
        decay_mm, mlpv_mm = sem("decay_mm"), sem("mlpv_mm")
        a_mix, proj_ev, turn_ev, exp_done, pt_ev = (sem("a_mix"), sem("proj_ev"), sem("turn_ev"), sem("exp_done"),
                                                    sem("pt_ev"))
        gate_out = [sem("gate_out0"), sem("gate_out1")]
        ctanh_done, lsig_ln, decay_done = sem("ctanh_done"), sem("lsig_ln"), sem("decay_done")
        v_mix, glu_done, rope_done, conv_done, cz_done, cn_done = (
            sem("v_mix"), sem("glu_done"), sem("rope_done"), sem("conv_done"), sem("cz_done"), sem("cn_done"))
        max_done, head_done, score_free, bias_done = sem("max_done"), sem("head_done"), sem("score_free"), sem("bias_done")
        lsig_min, rows_done, masked, mlh_done, mn_done = (sem("lsig_min"), sem("rows_done"), sem("masked"),
                                                          sem("mlh_done"), sem("mn_done"))
        mix_var, mix_rs = sem("mix_var"), sem("mix_rs")
        v_merge, bgh_done, branch_mm = sem("v_merge"), sem("bgh_done"), sem("branch_mm")
        gates_back = [sem("gates_back0"), sem("gates_back1")]
        gated, merged, out_mm, out_ev = sem("gated"), sem("merged"), sem("out_mm"), sem("out_ev")
        v_route, route_mm, route_diff, route_exp, assigned = (
            sem("v_route"), sem("route_mm"), sem("route_diff"), sem("route_exp"), sem("assigned"))
        rank_mm, slots_done, table_done, ffn_row_in = sem("rank_mm"), sem("slots_done"), sem("table_done"), sem("ffn_row")
        block_in = [sem("block_in0"), sem("block_in1")]
        xt_mm, xt_ev, up_mm, th_done = sem("xt_mm"), sem("xt_ev"), sem("up_mm"), sem("th_done")
        v_exp, hid_done, hid_mm, hid_ev = sem("v_exp"), sem("hid_done"), sem("hid_mm"), sem("hid_ev")
        down_mm, y_ev, y_out = sem("down_mm"), sem("y_ev"), [sem("y_out0"), sem("y_out1")]
        results_out = sem("results_out")
        y_free = sem("y_free")

        with nc.Block() as block:
            @block.sync
            def _(sp):
                sp.dma_start(consts[:, :], consts_in).then_inc(inputs_in, 16)
                sp.dma_start(x[:, 0:2, :], x_prompt.rearrange("b (t p) d -> p (b t) d", p=P)).then_inc(inputs_in, 16)
                sp.dma_start(x[:, 2:6, :], x_sample.rearrange("b (t p) d -> p (b t) d", p=P)).then_inc(inputs_in, 16)
                sp.wait_ge(inputs_in, 48)

            @block.scalar
            def _(act):
                act.wait_ge(inputs_in, 48)
                for b in range(BLOCKS):
                    act.dma_start(blocks[b * P:(b + 1) * P, :], x[:, b % T, :]).then_inc(rows_init, 16)

            @block.gpsimd
            def _(pool):
                pool.memset(nhalf, -0.5).then_inc(setup_done, 1)
                pool.memset(ones[:, :], 1.0).then_inc(setup_done, 1)
                pool.memset(cvx[:, :, :], 0.0).then_inc(setup_done, 1)
                pool.wait_ge(setup_done, 3)

        def normalised(name, read_params, turned, register):
            a_chain, sq_done, var_done, rs_done, h_done, ht_mm, ht_ev = (
                register(f"{name}_{s}") for s in ("chain", "sq", "var", "rs", "h", "ht_mm", "ht_ev"))
            rows_kept = turned == PP_GFFN
            hb = h_rows if rows_kept else reg_a[:, 0:2 * D].rearrange("p (s d) -> p s d", s=2)
            nb = T if rows_kept else 2
            squares = reg_a[:, 2 * D:3 * D]
            gain_row = reg_a[:, 3 * D:4 * D]
            with nc.Block() as block:
                @block.sync
                def _(sp):
                    read_params(sp)
                    if turned is None:
                        for t in range(T):
                            sp.wait_ge(h_done, t + 1)
                            y, r = (y_prompt, t) if t < 2 else (y_sample, t - 2)
                            sp.dma_start(y[0, r * P:(r + 1) * P, :], hb[:, t % 2, :]).then_inc(stored[t % 2], 16)
                        for s in range(2):
                            sp.wait_ge(stored[s], 16 * (T // 2))

                @block.scalar
                def _(act):
                    done = Tally(act, a_chain)
                    for t in range(T):
                        done(activate(squares, x[:, t, :], ACT.Square, accum_out=msq[:, t:t + 1]),
                             sq_done if t == T - 1 else a_chain)

                @block.gpsimd
                def _(pool):
                    pool.wait_ge(var_done, 1)
                    nc.gpsimd.tensor_tensor(rstd[:, 0:T], msq[:, 8:8 + T], nhalf[:, 0:T], ALU.pow).then_inc(rs_done, 1)

                @block.vector
                def _(dve):
                    dve.wait_ge(sq_done, 1)
                    ts_(msq[:, 8:8 + T], msq[:, 0:T], 1.0 / D, EPS, ALU.mult, ALU.add).then_inc(var_done, 1)
                    dve.wait_ge(rs_done, 1)
                    if turned is None:
                        dve.wait_ge(inputs_in, 64)
                    elif rows_kept:
                        dve.wait_ge(ffn_row_in, 16)
                    else:
                        dve.wait_ge(params_in, 32)

                    def scale(t):
                        if t >= nb and turned is not None:
                            dve.wait_ge(ht_mm, 2 * (t - 1))
                        if t >= 2 and turned is None:
                            dve.wait_ge(stored[t % 2], 16 * (t // 2))
                        if turned is None or rows_kept:
                            stt(hb[:, t % nb, :], x[:, t, :], rstd[:, t:t + 1], gain_row, ALU.mult,
                                ALU.mult).then_inc(h_done, 1)
                        else:
                            ts_(hb[:, t % 2, :], x[:, t, :], rstd[:, t:t + 1], None, ALU.mult).then_inc(h_done, 1)

                    scale(0)
                    for t in range(T):
                        if t + 1 < T:
                            scale(t + 1)
                        for q in range(2 if turned is not None else 0):
                            dve.wait_ge(ht_mm, 2 * t + q + 1)
                            if rows_kept:
                                nc.vector.tensor_copy(hT[:, 4 * q:4 * q + 4, t * P:(t + 1) * P],
                                                      bank[(2 * t + q) % 4][:, :].rearrange("p (k c) -> p k c", k=4)
                                                      ).then_inc(ht_ev, 1)
                                continue
                            tt(hT[:, 4 * q:4 * q + 4, t * P:(t + 1) * P],
                               bank[(2 * t + q) % 4][:, :].rearrange("p (k c) -> p k c", k=4),
                               pp[:, turned + 4 * q:turned + 4 * q + 4].unsqueeze(2).to_broadcast([P, 4, P]),
                               ALU.mult).then_inc(ht_ev, 1)

                if turned is None:
                    return

                @block.tensor
                def _(pe):
                    for t in range(T):
                        pe.wait_ge(h_done, t + 1)
                        for q in range(2):
                            if t >= 2:
                                pe.wait_ge(ht_ev, 2 * t + q - 3)
                            for k in range(4):
                                mm = nc.tensor.transpose(bank[(2 * t + q) % 4][:, k * P:(k + 1) * P],
                                                         hb[:, t % nb, (4 * q + k) * P:(4 * q + k + 1) * P], ident)
                            mm.then_inc(ht_mm, 1)

        def load_chunk(sp, layer, c):
            sp.dma_start(ring[:, c % 2, :], wd[bass.ds(layer * CHUNKS + c, 1)].rearrange("a p n -> (a p) n")
                         ).then_inc(chunk_in[c % 2], 16)

        def wait_chunk(pe, c):
            pe.wait_ge(chunk_in[c % 2], 16 * (c // 2 + 1))

        def score_bank(pe, s):
            if s >= 2:
                if s - 2 < ATT_UNITS:
                    pe.wait_ge(exp_done, s - 1)
                else:
                    pe.wait_ge(score_free, s - 1 - ATT_UNITS)

        def mix_tensor(pe):
            def proj(i, name, u):
                c = chunk_of(name, u)
                w = ring[:, c % 2, :].rearrange("p (k n) -> p k n", k=KD)
                wait_chunk(pe, c)
                if i >= 2:
                    pe.wait_ge(proj_ev, i - 1)
                for k in range(KD):
                    st = dict(start=(k == 0), stop=(k == KD - 1))
                    if name in ("cv", "na", "ml", "mg", "gate"):
                        j, hf = (u // 2 % 4, u % 2) if name != "mg" else (2, u)
                        mm = nc.tensor.matmul(bank[i % 2][:, 0:HALF], w[:, k, j * P:(j + 1) * P],
                                              hT[:, k, hf * HALF:(hf + 1) * HALF], **st)
                    else:
                        n = BW if name == "mo" else 512
                        mm = nc.tensor.matmul(bank[i % 2][:, 0:n], hT[:, k, u * P:(u + 1) * P], w[:, k, 0:n], **st)
                mm.then_inc(proj_mm, 1)

            def score(i, name, tile, h):
                first, n = GROUPS[tile_group(tile)]
                tq, tk = slice(tile * P, (tile + 1) * P), slice(first * P, (first + n) * P)
                score_bank(pe, i)
                if name == "at":
                    pe.wait_ge(turn_ev, at[("turn", "qk", first + n - 1)] + 1)
                    part = slice(HD * (h // 2), HD * (h // 2) + HD)
                    q, k = att[part, h % 2, tq], att[part, 2, tk]
                else:
                    pe.wait_ge(proj_ev, at[("proj", "nv", T - 1)] + 1)
                    part = slice(HD * (h % 2), HD * (h % 2) + HD)
                    q, k = naqk[part, h // 2, tq], naqk[part, 2 + h // 2, tk]
                nc.tensor.matmul(bank[4 + i % 2][:, 0:n * P], q, k, start=True, stop=True).then_inc(score_mm, 1)

            def ptrans(i, name, tile, h):
                n = GROUPS[tile_group(tile)][1]
                pe.wait_ge(exp_done, i + 1)
                if i >= 1:
                    pe.wait_ge(pt_ev, i)
                for k in range(n):
                    mm = nc.tensor.transpose(bank[6][:, k * P:(k + 1) * P], prob[:, i % 2, k * P:(k + 1) * P], ident)
                mm.then_inc(pt_mm, 1)

            def attend(i, name, tile, h):
                first, n = GROUPS[tile_group(tile)]
                pe.wait_ge(pt_ev, i + 1)
                if i >= 1:
                    pe.wait_ge(head_done, i)
                for k in range(n):
                    v = (atr[:, first + k, 384 + HD * (h // 2):384 + HD * (h // 2) + HD] if name == "at"
                         else nav[:, first + k, HD * h:HD * h + HD])
                    mm = nc.tensor.matmul(bank[7][:, HD * h:HD * h + HD], probT[:, i % 2, k * P:(k + 1) * P],
                                          v, start=(k == 0), stop=(k == n - 1))
                mm.then_inc(pv_mm, 1)

            def turn(i, name, t):
                if i >= 1:
                    pe.wait_ge(turn_ev, i)
                if name == "qk":
                    pe.wait_ge(rope_done, 1)
                    parts = [atr[:, t, j * P:(j + 1) * P] for j in range(3)]
                elif name == "cy":
                    pe.wait_ge(conv_done, 1)
                    first, _, off = SEGS[tile_group(t)]
                    o = off + t * P - first
                    parts = [cvy[:, j, o:o + P] for j in range(2)]
                elif name == "am":
                    pe.wait_ge(rows_done, 1)
                    parts = [am_rows[:, t * P:(t + 1) * P]]
                else:
                    if name == "cv":
                        pe.wait_ge(cn_done, 1)
                        o = cvz[:, t, :]
                    elif name == "ml":
                        pe.wait_ge(mn_done, 1)
                        o = hm[:, t, :]
                    else:
                        pe.wait_ge(head_done, at[("attend", name, t, HEADS - 1)] + 1)
                        o = outb[:, t % 2, :]
                    parts = [o[:, 0:P], o[:, P:BW]]
                for j, part in enumerate(parts):
                    mm = nc.tensor.transpose(bank[3][:, j * P:(j + 1) * P], part, ident)
                mm.then_inc(turn_mm, 1)

            def decay(i, g, h, d):
                first, n = GROUPS[g]
                pe.wait_ge(rows_done, 1)
                if i:
                    pe.wait_ge(decay_done, i)
                nc.tensor.matmul(bank[2][:, 0:n * P], ident[0:64, 32 * d + h:32 * d + h + 1].to_broadcast([64, P]),
                                 top_rows[0:64, first * P:(first + n) * P], start=True, stop=True).then_inc(decay_mm, 1)

            s_next = units_of["score"]

            def ml(i, g, h):
                nonlocal s_next
                first, n = GROUPS[g]
                tk = slice(first * P, (first + n) * P)
                pe.wait_ge(proj_ev, at[("proj", "mg", 1)] + 1)
                part = slice(HD * (h % 2), HD * (h % 2) + HD)
                for j in range(n):
                    score_bank(pe, s_next)
                    nc.tensor.matmul(bank[4 + s_next % 2][:, 0:n * P],
                                     mlqk[part, 2 + h // 2, (first + j) * P:(first + j + 1) * P],
                                     mlqk[part, h // 2, tk], start=True, stop=True).then_inc(score_mm, 1)
                    s_next += 1
                pe.wait_ge(score_free, s_next - ATT_UNITS)
                if i == 0:
                    pe.wait_ge(pt_ev, units_of["attend"])
                    pe.wait_ge(head_done, units_of["attend"])
                else:
                    pe.wait_ge(mlh_done, i)
                for d in range(2):
                    for t in range(n):
                        js = range(t + 1) if d == 0 else range(t, n)
                        for j in js:
                            mm = nc.tensor.matmul(bank[6 + d][:, 65 * t:65 * t + 65], mlw[:, d, j, t * P:(t + 1) * P],
                                                  mlv[:, first + j, h, :], start=(j == js[0]), stop=(j == js[-1]))
                mm.then_inc(mlpv_mm, 1)

            for kind, i, key in steps:
                if kind in ("proj", "score", "ptrans", "attend", "turn", "decay", "ml"):
                    {"proj": proj, "score": score, "ptrans": ptrans, "attend": attend, "turn": turn,
                     "decay": decay, "ml": ml}[kind](i, *key)

        def mix_scalar(act):
            done = Tally(act, a_mix)
            act.wait_ge(bgh_done, 1)
            at_over = at[("attend", "at", T - 1, HEADS - 1)] + 1

            def proj(i, name, u):
                b, half, j = bank[i % 2], slice((u % 2) * HALF, (u % 2 + 1) * HALF), u // 2
                act.wait_ge(proj_mm, i + 1)
                if name == "na" and u == 0:
                    act.wait_ge(turn_mm, at[("turn", "cv", T - 1)] + 1)
                if name in ("nv", "ml") and u == 0:
                    act.wait_ge(pv_mm, at_over)
                if name == "gate":
                    m, n, pair = u // (2 * NBR), u // 2 % NBR, u // 2
                    if pair >= 2 and u % 2 == 0:
                        act.wait_ge(gate_out[pair % 2], 16 * (pair // 2))
                    ins = activate(gbuf[:, pair % 2, half], b[:, 0:HALF], ACT.Tanh, scale=0.5,
                                   bias=bg_half[:, NBR * m + n:NBR * m + n + 1])
                elif name == "cv" and j < 2:
                    ins = activate(cvag[:, j, half], b[:, 0:HALF], ACT.Copy, scale=0.5)
                elif name == "cv":
                    ins = activate(cvag[:, j, half], b[:, 0:HALF], ACT.Tanh, scale=0.5)
                elif name == "na":
                    ins = activate(naqk[:, j, half], b[:, 0:HALF], ACT.Copy, scale=HD ** -0.5 if j < 2 else 1.0)
                elif name == "ml":
                    ins = activate(mlqk[:, j, half], b[:, 0:HALF], ACT.Copy, scale=1.0 if j < 2 else HD ** -0.5)
                elif name == "mg":
                    ins = activate(top_rows[:, half], b[:, 0:HALF], ACT.Identity, bias=pp[:, PP_GB:PP_GB + 1])
                elif name == "at":
                    ins = activate(atr[:, u, :], b[:, :], ACT.Copy)
                elif name == "mo":
                    ins = activate(mlo[:, u, :], b[:, 0:BW], ACT.Tanh, scale=0.5)
                else:
                    done(activate(nav[:, u, :], b[:, 0:BW], ACT.Copy))
                    done(activate(mlv[:, u, :, HD], ones[:, 0:HEADS], ACT.Copy))
                    ins = activate(mlv[:, u, :, 0:HD], b[:, BW:2 * BW].rearrange("p (h c) -> p h c", h=HEADS), ACT.Copy)
                done(ins, proj_ev)
                if name == "gate" and u % 2 == 1:
                    act.dma_start(gate_dram[u // 2], gbuf[:, u // 2 % 2, :]).then_inc(gate_out[u // 2 % 2], 16)

            def exp(i, name, tile, h):
                S = GROUPS[tile_group(tile)][1] * P
                act.wait_ge(max_done, i + 1)
                if i >= 2:
                    act.wait_ge(pt_mm, i - 1)
                    act.wait_ge(head_done, i - 1)
                src = bank[4 + i % 2][:, 0:S] if name == "at" else prob[:, i % 2, 0:S]
                done(activate(prob[:, i % 2, 0:S], src, ACT.Exp, bias=negm[:, i % 2:i % 2 + 1],
                              accum_out=rsum[:, i % 2:i % 2 + 1]), exp_done)

            def ptrans(i, name, tile, h):
                S = GROUPS[tile_group(tile)][1] * P
                act.wait_ge(pt_mm, i + 1)
                if i >= 2:
                    act.wait_ge(pv_mm, i - 1)
                done(activate(probT[:, i % 2, 0:S], bank[6][:, 0:S], ACT.Copy), pt_ev)

            def turn(i, name, t):
                act.wait_ge(turn_mm, i + 1)
                tok = slice(t * P, (t + 1) * P)
                two = bank[3][:, 0:2 * P].rearrange("p (j c) -> p j c", j=2)
                if name == "qk":
                    done(activate(att[:, 0:2, tok], two, ACT.Copy, scale=HD ** -0.5))
                    ins = activate(att[:, 2, tok], bank[3][:, 2 * P:3 * P], ACT.Copy)
                elif name == "cy":
                    ins = activate(cvz[:, t, :], bank[3][:, 0:BW], ACT.Copy)
                elif name == "am":
                    q = bank[3][:, 0:P].rearrange("p (q r) -> p q r", q=4)
                    done(activate(am[:, t, :, :], q[:, 0:2, 0:HEADS], ACT.Copy))
                    ins = activate(em[:, t, :, :], q[:, 2:4, 0:HEADS], ACT.Exp, scale=-1.0)
                else:
                    n = {"na": 0, "ml": 1, "cv": 2, "at": 3}[name]
                    ins = activate(oT[:, 2 * n:2 * n + 2, tok], two, ACT.Copy, scale=0.5 if name == "cv" else 1.0)
                done(ins, turn_ev)

            def gates():
                act.wait_ge(lsig_min, 1)
                r = sum_rows[0:64, :]
                done(activate(r, top_rows[64:128, :], ACT.Abs))
                done(activate(r, r, ACT.Exp, scale=-1.0))
                done(activate(r, r, ACT.Ln, bias=1.0), lsig_ln)

            def decay(i, g, h, d):
                first, n = GROUPS[g]
                S = n * P
                if i == 0:
                    act.wait_ge(score_free, ATT_UNITS)
                elif d == 0:
                    act.wait_ge(mlpv_mm, i // 2)
                if True:
                    act.wait_ge(masked, i + 1)
                    for j in range(n):
                        a = am[:, first + j, d, h:h + 1]
                        lo, hi = ((j + 1) * P, S) if d == 0 else (0, j * P)
                        if hi > lo:
                            done(activate(mlw[:, d, j, lo:hi], bank[2][:, lo:hi], ACT.Exp, bias=a, scale=-1.0))
                        ins = activate(mlw[:, d, j, j * P:(j + 1) * P], dg[:, j * P:(j + 1) * P], ACT.Exp, bias=a,
                                       scale=-1.0)
                        done(ins, decay_done if j == n - 1 else None)

            def cnorm(i):
                act.wait_ge(cz_done, 1)
                done(activate(cvt, cvz, ACT.Tanh, scale=0.5), ctanh_done)

            for kind, i, key in steps:
                if kind == "gates":
                    gates()
                elif kind in ("proj", "exp", "ptrans", "turn", "decay", "cnorm"):
                    {"proj": proj, "exp": exp, "ptrans": ptrans, "turn": turn, "decay": decay,
                     "cnorm": cnorm}[kind](i, *key)

        def mix_vector(dve):
            done = Tally(dve, v_mix)
            done(ts_(bg_half, pp[:, PP_BG:PP_BG + 32], 0.5, None, ALU.mult), bgh_done)
            h4 = lambda a: a.rearrange("p t (h d) -> p t h d", d=HD)
            row = lambda o, n: rows[:, o:o + n].unsqueeze(1).to_broadcast([P, T, n])

            def glu(i):
                dve.wait_ge(proj_ev, at[("proj", "cv", 7)] + 1)
                for lo, n, off in SEGS:
                    done(stt(cvx[:, :, PAD + off:PAD + off + n], cvag[:, 2:4, lo:lo + n], 1.0,
                             cvag[:, 0:2, lo:lo + n], ALU.add, ALU.mult))

            def conv(i):
                for k in range(TAPS * i // ATT_UNITS, TAPS * (i + 1) // ATT_UNITS):
                    for j in range(2):
                        w, y, src = pp[:, PP_CW + TAPS * j + k:PP_CW + TAPS * j + k + 1], cvy[:, j, :], cvx[
                            :, j, k:k + CONV_OUT]
                        last = conv_done if (k, j) == (TAPS - 1, 1) else None
                        if k == 0:
                            done(ts_(y, src, w, pp[:, PP_CB + j:PP_CB + j + 1], ALU.mult, ALU.add), last)
                        else:
                            done(stt(y, src, w, y, ALU.mult, ALU.add), last)

            def rope(i):
                dve.wait_ge(proj_ev, at[("proj", "at", T - 1)] + 1)
                qk = atr[:, :, 0:384]
                done(tt(rope_tmp, qk, qk, ALU.mult))
                done(reduce_(msq[:, 0:36].rearrange("p (t h) -> p t h", t=T), h4(rope_tmp), AX.X, ALU.add))
                done(ts_(msq[:, 0:36], msq[:, 0:36], 1.0 / HD, EPS, ALU.mult, ALU.add), mix_var)
                dve.wait_ge(mix_rs, 1)
                r = rstd[:, 0:36].rearrange("p (t h) -> p t h", t=T).unsqueeze(3).to_broadcast([P, T, 6, HD])
                done(tt(h4(qk), h4(qk), r, ALU.mult))
                done(tt(qk, qk, row(R_ATT, 384), ALU.mult))
                for a in range(4):
                    o, other = 16 * a, 16 * (a ^ 1)
                    s = sin[:, :, o:o + 16].unsqueeze(2).to_broadcast([P, T, 6, 16])
                    done(tt(h4(rope_tmp)[:, :, :, o:o + 16], h4(qk)[:, :, :, other:other + 16], s, ALU.mult))
                done(tt(h4(qk), h4(qk), cos.unsqueeze(2).to_broadcast([P, T, 6, HD]), ALU.mult))
                done(tt(qk, qk, rope_tmp, ALU.add), rope_done)

            def score(i, name, tile, h):
                S = GROUPS[tile_group(tile)][1] * P
                s, m = bank[4 + i % 2][:, 0:S], negm[:, i % 2:i % 2 + 1]
                dve.wait_ge(score_mm, i + 1)
                if i >= 2:
                    dve.wait_ge(exp_done, i - 1)
                if name == "na":
                    dve.wait_ge(pt_mm, i - 1)
                    r = tile - GROUPS[tile_group(tile)][0]
                    grid = lambda a: a.rearrange("p (r c) -> p r c", c=GRID)
                    done(tt(grid(prob[:, i % 2, 0:S]), grid(s), bias_tab[:, h, 7 - 2 * r:7 - 2 * r + S // GRID, :],
                            ALU.add), score_free)
                    s = prob[:, i % 2, 0:S]
                done(reduce_(m, s, AX.X, ALU.max, negate=True), max_done)

            def attend(i, name, tile, h):
                dve.wait_ge(exp_done, i + 1)
                done(nc.vector.reciprocal(rrec, rsum[:, i % 2:i % 2 + 1]))
                dve.wait_ge(pv_mm, i + 1)
                if h == 0 and (name, tile) not in (("at", 0), ("at", 1)):
                    prev = (name, tile - 2) if tile >= 2 else ("at", tile + 4)
                    dve.wait_ge(turn_mm, at[("turn", *prev)] + 1)
                done(ts_(outb[:, tile % 2, HD * h:HD * h + HD], bank[7][:, HD * h:HD * h + HD], rrec, None, ALU.mult),
                     head_done)

            def cnorm(i):
                dve.wait_ge(turn_ev, at[("turn", "cy", T - 1)] + 1)
                z, per_token = cvz, lambda a: a.unsqueeze(2).to_broadcast([P, T, BW])
                done(reduce_(lmean, z, AX.X, ALU.add))
                done(ts_(lmean, lmean, 1.0 / BW, None, ALU.mult))
                done(tt(z, z, per_token(lmean), ALU.subtract))
                done(tt(cvt, z, z, ALU.mult))
                done(reduce_(msq[:, 0:T], cvt, AX.X, ALU.add))
                done(ts_(msq[:, 0:T], msq[:, 0:T], 1.0 / BW, EPS, ALU.mult, ALU.add), mix_var)
                dve.wait_ge(mix_rs, 2)
                done(tt(z, z, per_token(rstd[:, 0:T]), ALU.mult))
                done(tt(z, z, row(R_CG, BW), ALU.mult))
                done(tt(z, z, row(R_CB, BW), ALU.add), cz_done)
                dve.wait_ge(ctanh_done, 1)
                done(stt(z, cvt, 1.0, z, ALU.add, ALU.mult), cn_done)

            def bias(i):
                dve.wait_ge(bias_in_sem, 16)
                t = wide[:, :].rearrange("p (a c) -> p a c", c=GRID)
                done(tt(t, t, win.unsqueeze(1).to_broadcast([P, CW // GRID, GRID]), ALU.add), bias_done)

            def gates():
                fw, bw = slice(0, 32), slice(32, 64)
                dve.wait_ge(proj_ev, at[("proj", "mg", 1)] + 1)
                done(ts_(am_rows[0:64, :], top_rows[64:128, :], 0.0, None, ALU.min), lsig_min)
                dve.wait_ge(lsig_ln, 1)
                done(tt(am_rows[0:64, :], am_rows[0:64, :], sum_rows[0:64, :], ALU.subtract))
                for g, (first, n) in enumerate(GROUPS):
                    lo, S = first * P, n * P
                    seg = slice(lo, lo + S)
                    done(scan(sum_rows[0:64, seg], ones[0:64, 0:1].to_broadcast([64, S]), am_rows[0:64, seg], 0.0, ALU.mult, ALU.add))
                    done(nc.vector.tensor_copy(dg[bw, 1:S], sum_rows[bw, lo:lo + S - 1]))
                    done(nc.vector.memset(dg[bw, 0:1], 0.0))
                    done(tt(am_rows[fw, seg], top_rows[fw, seg], sum_rows[fw, seg], ALU.subtract))
                    done(tt(am_rows[bw, seg], top_rows[bw, seg], dg[bw, 0:S], ALU.add))
                    done(scan(top_rows[fw, seg], am_rows[fw, seg], am_rows[fw, seg], NEG, ALU.max, ALU.max))
                    back = am_rows[bw, seg][:, ::-1]
                    done(scan(top_rows[bw, seg][:, ::-1], back, back, NEG, ALU.max, ALU.max))
                    done(tt(am_rows[64:96, seg], top_rows[fw, seg], sum_rows[fw, seg], ALU.add))
                    done(tt(am_rows[96:128, seg], top_rows[bw, seg], dg[bw, 0:S], ALU.subtract),
                         rows_done if g == 1 else None)

            s_next = units_of["score"]

            def decay(i, g, h, d):
                n = GROUPS[g][1]
                S = n * P
                dve.wait_ge(decay_mm, i + 1)
                if i:
                    dve.wait_ge(decay_done, i)
                blocks = lambda a: a.rearrange("p (j c) -> p j c", c=P)
                done(tt(blocks(dg[:, 0:S]), blocks(bank[2][:, 0:S]),
                        tri[:, d, :].unsqueeze(1).to_broadcast([P, n, P]), ALU.add), masked)

            def ml(i, g, h):
                nonlocal s_next
                first, n = GROUPS[g]
                S = n * P
                dve.wait_ge(decay_done, 2 * i + 2)
                for j in range(n):
                    dve.wait_ge(score_mm, s_next + 1)
                    b = bank[4 + s_next % 2]
                    s_next += 1
                    w0, w1 = mlw[:, 0, j, j * P:S], mlw[:, 1, j, 0:(j + 1) * P]
                    done(tt(w0, b[:, j * P:S], w0, ALU.mult))
                    done(tt(w1, b[:, 0:(j + 1) * P], w1, ALU.mult), score_free)
                dve.wait_ge(turn_ev, at[("turn", "am", T - 1)] + 1)
                dve.wait_ge(mlpv_mm, i + 1)
                num = [bank[6 + d][:, 0:65 * n].rearrange("p (t c) -> p t c", c=65) for d in range(2)]
                for d in range(2):
                    done(nc.vector.tensor_copy(den[:, d, 0:n], num[d][:, :, HD]))
                done(stt(den2[:, :, 0:n], den[:, :, 0:n], -1.0, den[:, :, 0:n], ALU.mult, ALU.max))
                e = em[:, first:first + n, :, h].rearrange("p t d -> p d t")
                done(tt(den2[:, :, 0:n], den2[:, :, 0:n], e, ALU.max))
                done(nc.vector.reciprocal(den[:, :, 0:n], den2[:, :, 0:n]))
                o, tmp = hm[:, first:first + n, HD * h:HD * h + HD], dg[:, 0:HD * n].rearrange("p (t c) -> p t c", c=HD)
                r = [den[:, d, 0:n].unsqueeze(2).to_broadcast([P, n, HD]) for d in range(2)]
                done(tt(o, num[0][:, :, 0:HD], r[0], ALU.mult))
                done(tt(tmp, num[1][:, :, 0:HD], r[1], ALU.mult))
                done(tt(o, o, tmp, ALU.add), mlh_done)

            def mnorm(i):
                sq = wide[:, 0:1536].rearrange("p (t c) -> p t c", t=T)
                done(tt(sq, hm, hm, ALU.mult))
                done(reduce_(msq[:, 0:24].rearrange("p (t h) -> p t h", t=T), h4(sq), AX.X, ALU.add))
                done(ts_(msq[:, 0:24], msq[:, 0:24], 1.0 / HD, EPS, ALU.mult, ALU.add), mix_var)
                dve.wait_ge(mix_rs, 3)
                done(ts_(rstd[:, 0:24], rstd[:, 0:24], 0.5, None, ALU.mult))
                r = rstd[:, 0:24].rearrange("p (t h) -> p t h", t=T).unsqueeze(3).to_broadcast([P, T, HEADS, HD])
                done(tt(h4(hm), h4(hm), r, ALU.mult))
                done(tt(hm, hm, row(R_ML, BW), ALU.mult))
                done(stt(hm, mlo, 1.0, hm, ALU.add, ALU.mult), mn_done)

            for kind, i, key in steps:
                if kind == "gates":
                    gates()
                elif kind in ("glu", "rope", "conv", "cnorm", "bias", "score", "attend", "decay", "ml", "mnorm"):
                    {"glu": glu, "rope": rope, "conv": conv, "cnorm": cnorm, "bias": bias, "score": score,
                     "attend": attend, "decay": decay, "ml": ml, "mnorm": mnorm}[kind](i, *key)

        def mix(layer):
            with nc.Block() as block:
                @block.sync
                def _(sp):
                    for c in range(MIX_CHUNKS):
                        if c >= 2:
                            sp.wait_ge(proj_mm, last_proj[c - 2] + 1)
                        load_chunk(sp, layer, c)
                        if c == 1:
                            sp.dma_start(wide[:, :], bias_in[bass.ds(layer, 1)].rearrange("a p n -> (a p) n")
                                         ).then_inc(bias_in_sem, 16)

                @block.gpsimd
                def _(pool):
                    for r, n in enumerate([36, T, 24]):
                        pool.wait_ge(mix_var, r + 1)
                        nc.gpsimd.tensor_tensor(rstd[:, 0:n], msq[:, 0:n], nhalf[:, 0:n], ALU.pow).then_inc(mix_rs, 1)

                block.tensor(mix_tensor)
                block.scalar(mix_scalar)
                block.vector(mix_vector)

        def merge(layer):
            units = [(m, n, hf) for m in range(KD) for n in range(NBR) for hf in range(2)]
            half = [slice(0, HALF), slice(HALF, TOK)]
            wb_sb = [wide[:, :].rearrange("p (n k c) -> p n k c", n=NBR, k=2),
                     reg_a[:, 0:CW].rearrange("p (n k c) -> p n k c", n=NBR, k=2)]
            with nc.Block() as block:
                @block.sync
                def _(sp):
                    for c in range(2):
                        sp.dma_start((wide[:, :], reg_a[:, 0:CW])[c], wb[bass.ds(layer * 2 + c, 1)]
                                     .rearrange("a p n -> (a p) n")).then_inc(wb_in[c], 16)
                    for s in range(2):
                        sp.wait_ge(gate_out[s], 16 * GATE_UNITS // 4)
                    for m in range(KD):
                        if m >= 2:
                            sp.wait_ge(gated, 8 * (m - 1))
                        sp.dma_start(ring[:, m % 2, 0:NBR * TOK].rearrange("p (n t) -> p n t", n=NBR),
                                     gate_dram[NBR * m:NBR * (m + 1)].rearrange("n p t -> p n t")
                                     ).then_inc(gates_back[m % 2], 16)
                    sp.dma_start(wr_sb[:, :, :].rearrange("p k n -> p (k n)"),
                                 wr[bass.ds(layer, 1)].rearrange("a p n -> (a p) n")).then_inc(wr_in, 16)
                    for c in range(MIX_CHUNKS, CHUNKS):
                        sp.wait_ge(gated, 8 * (KD - 1 + c - MIX_CHUNKS))
                        load_chunk(sp, layer, c)

                @block.tensor
                def _(pe):
                    for q, (m, n, hf) in enumerate(units):
                        pe.wait_ge(wb_in[m // 4], 16)
                        if q >= 8:
                            pe.wait_ge(gated, q - 7)
                        for k in range(2):
                            mm = nc.tensor.matmul(bank[q % 8][:, 0:HALF],
                                                  wb_sb[m // 4][:, n, k, (m % 4) * P:(m % 4 + 1) * P],
                                                  oT[:, 2 * n + k, half[hf]], start=(k == 0), stop=(k == 1))
                        mm.then_inc(branch_mm, 1)
                    pe.wait_ge(merged, 2 * KD)
                    for o in range(2 * T):
                        c, t = MIX_CHUNKS + o // T, o % T
                        w = ring[:, c % 2, :].rearrange("p (k n) -> p k n", k=KD)
                        wait_chunk(pe, c)
                        if o >= 4:
                            pe.wait_ge(out_ev, o - 3)
                        for k in range(KD):
                            mm = nc.tensor.matmul(bank[o % 4][:, :], mT[:, k, t * P:(t + 1) * P], w[:, k, :],
                                                  start=(k == 0), stop=(k == KD - 1))
                        mm.then_inc(out_mm, 1)

                @block.vector
                def _(dve):
                    done = Tally(dve, v_merge)
                    dve.wait_ge(rows_init, 16 * BLOCKS)
                    for q, (m, n, hf) in enumerate(units):
                        dve.wait_ge(gates_back[m % 2], 16 * (m // 2 + 1))
                        dve.wait_ge(branch_mm, q + 1)
                        gate = ring[:, m % 2, n * TOK + hf * HALF:n * TOK + (hf + 1) * HALF]
                        to, tmp = mT[:, m, half[hf]], dg[:, 0:HALF]
                        done(stt(tmp if n else to, gate, 1.0, bank[q % 8][:, 0:HALF], ALU.add, ALU.mult), gated)
                        if n:
                            done(tt(to, to, tmp, ALU.add), merged if n == NBR - 1 else None)
                    for o in range(2 * T):
                        c, t = o // T, o % T
                        dve.wait_ge(out_mm, o + 1)
                        xs = x[:, t, c * 512:(c + 1) * 512]
                        done(stt(xs, bank[o % 4][:, :], 0.5, xs, ALU.mult, ALU.add), out_ev)

        def experts(layer):
            flat = hT[:, :, :].rearrange("p a b -> p (a b)")
            x_in = [flat[:, s * D:(s + 1) * D] for s in range(2)]
            xT = [flat[:, (2 + s) * D:(3 + s) * D].rearrange("p (k c) -> p k c", k=KD) for s in range(2)]
            y_sb = [flat[:, (4 + s) * D:(5 + s) * D] for s in range(2)]
            up_w = [slot_w[s][:, 0:KD * 2 * DE].rearrange("p (k n) -> p k n", k=KD) for s in range(2)]
            down_w = [slot_w[s][:, KD * 2 * DE:EW].rearrange("p (k n) -> p k n", k=2) for s in range(2)]
            hidb = [prob[:, s, 0:DE] for s in range(2)]
            thb = [prob[:, s, DE:2 * DE] for s in range(2)]
            hidT = [probT[:, s, 0:DE].rearrange("p (k c) -> p k c", k=2) for s in range(2)]
            ring_flat = ring[:, :, :].rearrange("p a b -> p (a b)")

            def y_back(t, c):
                i = TOP * t + c
                return ring_flat[:, i * D:(i + 1) * D] if i < 8 else wide[:, (i - 8) * D:(i - 7) * D]

            lg = rt[:, 0:120].rearrange("p (t e) -> p t e", t=T)
            g6 = lambda a: a.unsqueeze(2).to_broadcast([P, T, NG])
            col = lambda o: rt[:, o:o + T]
            four = lambda o: rt[:, o:o + 24].rearrange("p (t g) -> p t g", t=T)
            gl, el = lg[:, :, 0:NG], lg[:, :, NG:NG + NE]
            gmax, gsum, top1, top2, w1, w2, ex = (col(120 + 6 * i) for i in range(7))
            group_exp, group1, first1, first2, ein, masked_e, cand = (four(168 + 24 * i) for i in range(7))
            prod = rt[:, 336:432].rearrange("p (t g j) -> p t g j", t=T, g=NG)
            part = lambda o, n: reg_a[:, o:o + n]
            by_e = lambda a: a.rearrange("p (t e) -> p t e", t=T)
            one1, one2, both, where, over = (part(96 * i, 96) for i in range(5))
            rank, count = part(480, 96), part(576, NE)
            spare, spare_sum, jump = part(592, NE), part(608, NE), part(624, NE)
            slot_f = part(640, T * TOP).rearrange("p (t c) -> p t c", c=TOP)
            below = part(656, SPARE * NE).rearrange("p (j e) -> p j e", j=SPARE)
            table_f, more = part(848, SPARE + 1), part(864, SPARE // 2)

            with nc.Block() as block:
                @block.sync
                def _(sp):
                    sp.wait_ge(table_done, 1)
                    pairs = sp.value_load(table[0:1, SPARE:SPARE + 1], min_val=NE // 2 + 1, max_val=BLOCKS // 2)
                    sp.wait_ge(scattered, layer * (16 * T * TOP) + 16 * T * TOP)

                    def rows_of(pair, s):
                        sp.dma_start(x_in[s], blocks.rearrange("(b p) d -> b p d", p=P)[bass.ds(pair * 2 + s, 1)]
                                     .rearrange("a p d -> (a p) d")).then_inc(block_in[s], 16)

                    for s in range(2):
                        sp.dma_start(x_in[s], blocks[s * P:(s + 1) * P, :]).then_inc(block_in[s], 16)
                    with sp.Fori(1, NE // 2) as pair:
                        for s in range(2):
                            sp.wait_ge(down_mm, pair * 2 + s - 1)
                            rows_of(pair, s)
                            sp.dma_start(slot_w[s], we[bass.ds(layer * NE + pair * 2 + s, 1)]
                                         .rearrange("a p n -> (a p) n")).then_inc(expert_in[s], 16)
                    with sp.Fori(NE // 2, pairs) as pair:
                        for s in range(2):
                            e = sp.value_load(table[0:1, bass.ds((pair - NE // 2) * 2 + s, 1)], min_val=0,
                                              max_val=NE - 1)
                            sp.wait_ge(down_mm, pair * 2 + s - 1)
                            rows_of(pair, s)
                            sp.dma_start(slot_w[s], we[bass.ds(layer * NE + e, 1)]
                                         .rearrange("a p n -> (a p) n")).then_inc(expert_in[s], 16)

                @block.tensor
                def _(pe):
                    pe.wait_ge(wr_in, 16)
                    for t in range(T):
                        for k in range(KD):
                            mm = nc.tensor.matmul(bank[0][:, t * 20:(t + 1) * 20], hT[:, k, t * P:(t + 1) * P],
                                                  wr_sb[:, k, :], start=(k == 0), stop=(k == KD - 1))
                    mm.then_inc(route_mm, 1)
                    pe.wait_ge(assigned, 1)
                    every = ones[:, 0:1].to_broadcast([P, P])
                    for t in range(T + 1):
                        o = bank[1][:, NE * t:NE * (t + 1)]
                        for u in range(t):
                            mm = nc.tensor.matmul(o, every, both[:, NE * u:NE * (u + 1)], start=(u == 0),
                                                  stop=(t == T and u == T - 1))
                        if t < T:
                            mm = nc.tensor.matmul(o, before, both[:, NE * t:NE * (t + 1)], start=(t == 0), stop=True)
                    mm.then_inc(rank_mm, 1)
                    pe.wait_ge(table_done, 1)
                    pairs = pe.value_load(table[0:1, SPARE:SPARE + 1], min_val=NE // 2 + 1, max_val=BLOCKS // 2)
                    with pe.Fori(0, pairs) as pair:
                        b = lambda s, more: pair * 2 + (s + more)
                        for s in range(2):
                            pe.wait_ge(block_in[s], pair * 16 + 16)
                            pe.wait_ge(y_ev, b(s, 1))
                            for k in range(KD):
                                mm = nc.tensor.transpose(bank[2 + 2 * s + k // 4][:, (k % 4) * P:(k % 4 + 1) * P],
                                                         x_in[s][:, k * P:(k + 1) * P], ident)
                            mm.then_inc(xt_mm, 1)
                        for s in range(2):
                            pe.wait_ge(expert_in[s], pair * 16 + 16)
                            pe.wait_ge(xt_ev, b(s, 1))
                            pe.wait_ge(hid_done, b(s, 1))
                            for k in range(KD):
                                mm = nc.tensor.matmul(bank[s][:, :], xT[s][:, k, :], up_w[s][:, k, :],
                                                      start=(k == 0), stop=(k == KD - 1))
                            mm.then_inc(up_mm, 1)
                        for s in range(2):
                            pe.wait_ge(hid_done, b(s, 3))
                            pe.wait_ge(hid_ev, b(s, 1))
                            for k in range(2):
                                mm = nc.tensor.transpose(bank[6 + s][:, k * P:(k + 1) * P],
                                                         hidb[s][:, k * P:(k + 1) * P], ident)
                            mm.then_inc(hid_mm, 1)
                            pe.wait_ge(hid_ev, b(s, 3))
                            for c in range(2):
                                for k in range(2):
                                    mm = nc.tensor.matmul(bank[2 + 2 * s + c][:, :], hidT[s][:, k, :],
                                                          down_w[s][:, k, c * 512:(c + 1) * 512],
                                                          start=(k == 0), stop=(k == 1))
                            mm.then_inc(down_mm, 1)

                @block.scalar
                def _(act):
                    act.wait_ge(route_diff, 1)
                    activate(group_exp, group_exp, ACT.Exp).then_inc(route_exp, 1)
                    act.wait_ge(route_diff, 2)
                    activate(ex, ex, ACT.Exp).then_inc(route_exp, 1)
                    act.sem_inc(hid_ev, 2)
                    act.wait_ge(table_done, 1)
                    pairs = act.value_load(table[0:1, SPARE:SPARE + 1], min_val=NE // 2 + 1, max_val=BLOCKS // 2)
                    with act.Fori(0, pairs) as pair:
                        b = lambda s, more: pair * 2 + (s + more)
                        for s in range(2):
                            act.wait_ge(xt_mm, b(s, 1))
                            activate(xT[s][:, 0:4, :], bank[2 + 2 * s][:, :].rearrange("p (k c) -> p k c", k=4), ACT.Copy)
                            activate(xT[s][:, 4:8, :], bank[3 + 2 * s][:, :].rearrange("p (k c) -> p k c", k=4),
                                     ACT.Copy).then_inc(xt_ev, 1)
                        for s in range(2):
                            act.wait_ge(up_mm, b(s, 1))
                            act.wait_ge(hid_done, b(s, 1))
                            activate(thb[s], bank[s][:, 0:DE], ACT.Tanh, scale=0.5).then_inc(th_done, 1)
                        for s in range(2):
                            act.wait_ge(hid_mm, b(s, 1))
                            activate(hidT[s], bank[6 + s][:, 0:DE].rearrange("p (k c) -> p k c", k=2),
                                     ACT.Copy).then_inc(hid_ev, 1)
                        for s in range(2):
                            act.wait_ge(y_ev, b(s, 3))
                            act.dma_start(blocks.rearrange("(b p) d -> b p d", p=P)[bass.ds(pair * 2 + s, 1)]
                                          .rearrange("a p d -> (a p) d"), y_sb[s]).then_inc(y_out[s], 16)

                @block.gpsimd
                def _(pool):
                    pool.wait_ge(rows_init, 16 * BLOCKS)
                    pool.wait_ge(slots_done, 1)
                    for t in range(T):
                        for c in range(TOP):
                            i = TOP * t + c
                            pool.indirect_dma_start(
                                out=blocks, out_offset=bass.IndirectOffsetOnAxis(ap=slots[:, i:i + 1], axis=0),
                                in_=h_rows[:, t, :], in_offset=None).then_inc(scattered, 16)
                    pool.sem_inc(y_free, 2)
                    pool.wait_ge(table_done, 1)
                    pairs = pool.value_load(table[0:1, SPARE:SPARE + 1], min_val=NE // 2 + 1, max_val=BLOCKS // 2)
                    with pool.Fori(0, pairs) as pair:
                        for s in range(2):
                            pool.wait_ge(y_out[s], pair * 16 + 16)
                            pool.sem_inc(y_free, 1)
                    pool.sem_inc(results_out, 1)
                    pool.wait_ge(results_out, 1)
                    for t in range(T):
                        for c in range(TOP):
                            i = TOP * t + c
                            pool.indirect_dma_start(
                                out=y_back(t, c), out_offset=None, in_=blocks,
                                in_offset=bass.IndirectOffsetOnAxis(ap=slots[:, i:i + 1], axis=0)
                            ).then_inc(gathered[t], 16)

                @block.vector
                def _(dve):
                    done = Tally(dve, v_route)

                    def first_of(src, best, to):
                        done(tt(cand, src, g6(best), ALU.is_equal))
                        done(ts_(cand, cand, -16.0, 16.0, ALU.mult, ALU.add))
                        done(tt(cand, cand, iota[:, 0:NG].unsqueeze(1).to_broadcast([P, T, NG]), ALU.add))
                        done(reduce_(ex, cand, AX.X, ALU.min))
                        done(tt(to, cand, g6(ex), ALU.is_equal))

                    dve.wait_ge(route_mm, 1)
                    done(tt(lg, bank[0][:, 0:120].rearrange("p (t e) -> p t e", t=T),
                            rows[:, R_MOE:R_MOE + 20].unsqueeze(1).to_broadcast([P, T, 20]), ALU.add))
                    done(reduce_(gmax, gl, AX.X, ALU.max))
                    done(tt(group_exp, gl, g6(gmax), ALU.subtract), route_diff)
                    first_of(gl, gmax, group1)
                    by_group = group1.unsqueeze(3).to_broadcast([P, T, NG, 4])
                    done(tt(prod, el.rearrange("p t (g j) -> p t g j", g=NG), by_group, ALU.mult))
                    done(reduce_(ein, prod.rearrange("p t g j -> p t j g"), AX.X, ALU.add))
                    done(reduce_(top1, ein, AX.X, ALU.max))
                    first_of(ein, top1, first1)
                    done(stt(masked_e, first1, NEG, ein, ALU.mult, ALU.add))
                    done(reduce_(top2, masked_e, AX.X, ALU.max))
                    first_of(masked_e, top2, first2)
                    for one, first in ((one1, first1), (one2, first2)):
                        done(tt(one.rearrange("p (t g j) -> p t g j", t=T, g=NG), by_group,
                                first.unsqueeze(2).to_broadcast([P, T, NG, 4]), ALU.mult))
                    done(tt(both, one1, one2, ALU.add), assigned)
                    dve.wait_ge(route_exp, 1)
                    done(reduce_(gsum, group_exp, AX.X, ALU.add))
                    done(tt(ex, top2, top1, ALU.subtract), route_diff)
                    dve.wait_ge(route_exp, 2)
                    done(ts_(w1, ex, 1.0, 2.0, ALU.add, ALU.mult))
                    done(tt(w1, w1, gsum, ALU.mult))
                    done(nc.vector.reciprocal(w1, w1))
                    done(tt(w2, w1, ex, ALU.mult))

                    dve.wait_ge(rank_mm, 1)
                    done(nc.vector.tensor_copy(reg_a[:, 480:592], bank[1][:, 0:112]))
                    done(ts_(spare, count, float(P), None, ALU.is_gt))
                    for j in range(2, T):
                        done(stt(spare, count, float(P * j), spare, ALU.is_gt, ALU.add))
                    done(scan(spare_sum, ones[:, 0:1].to_broadcast([P, NE]), spare, 0.0, ALU.mult, ALU.add))
                    done(tt(jump, spare_sum, spare, ALU.subtract))
                    done(stt(jump, jump, float(P), e128, ALU.mult, ALU.subtract))
                    done(ts_(jump, jump, float(P * (NE - 1)), None, ALU.add))
                    per_e = lambda a: a.unsqueeze(1).to_broadcast([P, T, NE])
                    done(ts_(over, rank, float(P), None, ALU.is_ge))
                    done(tt(by_e(over), by_e(over), per_e(jump), ALU.mult))
                    done(tt(where, rank, over, ALU.add))
                    done(tt(by_e(where), by_e(where), per_e(e128), ALU.add))
                    for c, one in enumerate((one1, one2)):
                        done(tt(over, one, where, ALU.mult))
                        done(reduce_(slot_f[:, :, c], by_e(over), AX.X, ALU.add))
                    done(nc.vector.tensor_copy(slots[:, :].rearrange("p (t c) -> p t c", c=TOP), slot_f), slots_done)
                    done(tt(below, spare_sum.unsqueeze(1).to_broadcast([P, SPARE, NE]),
                            iota.unsqueeze(2).to_broadcast([P, SPARE, NE]), ALU.is_le))
                    done(reduce_(table_f[:, 0:SPARE], below, AX.X, ALU.add))
                    done(ts_(table_f[:, 0:SPARE], table_f[:, 0:SPARE], float(NE - 1), None, ALU.min))
                    done(ts_(more, iota[:, 0:SPARE // 2], 2.0, spare_sum[:, NE - 1:NE], ALU.mult, ALU.is_lt))
                    done(reduce_(table_f[:, SPARE:SPARE + 1], more, AX.X, ALU.add))
                    done(ts_(table_f[:, SPARE:SPARE + 1], table_f[:, SPARE:SPARE + 1], 1.0, float(NE // 2), ALU.max,
                             ALU.add))
                    done(nc.vector.tensor_copy(table[:, :], table_f), table_done)

                    dve.sem_inc(hid_done, 2)
                    dve.sem_inc(y_ev, 2)
                    pairs = dve.value_load(table[0:1, SPARE:SPARE + 1], min_val=NE // 2 + 1, max_val=BLOCKS // 2)
                    with dve.Fori(0, pairs) as pair:
                        b = lambda s, more: pair * 2 + (s + more)
                        for s in range(2):
                            dve.wait_ge(th_done, b(s, 1))
                            stt(thb[s], thb[s], 1.0, bank[s][:, 0:DE], ALU.add, ALU.mult).then_inc(v_exp, 1)
                            dve.wait_ge(v_exp, b(s, 1))
                            tt(hidb[s], bank[s][:, DE:2 * DE], thb[s], ALU.mult).then_inc(hid_done, 1)
                        for s in range(2):
                            dve.wait_ge(down_mm, b(s, 1))
                            dve.wait_ge(y_free, b(s, 1))
                            for c in range(2):
                                ins = nc.vector.tensor_copy(y_sb[s][:, c * 512:(c + 1) * 512], bank[2 + 2 * s + c][:, :])
                            ins.then_inc(y_ev, 1)
                    for t in range(T):
                        dve.wait_ge(gathered[t], layer * (16 * TOP) + 16 * TOP)
                        for c, w in enumerate((w1, w2)):
                            done(stt(x[:, t, :], y_back(t, c), w[:, t:t + 1], x[:, t, :], ALU.mult, ALU.add))

        def read_layer_params(layer):
            def read(sp):
                sp.dma_start(pp[:, :], pp_in[bass.ds(layer, 1)].rearrange("a p n -> (a p) n")).then_inc(params_in, 16)
                sp.dma_start(rows[:, :], rows_in[bass.ds(layer, 1), :].to_broadcast([P, R_N])).then_inc(params_in, 16)
            return read

        def read_first_experts(layer):
            def read(sp):
                sp.dma_start(reg_a[:, 3 * D:4 * D], ffn_in[bass.ds(layer, 1), :].to_broadcast([P, D])
                             ).then_inc(ffn_row_in, 16)
                for s in range(2):
                    sp.dma_start(slot_w[s], we[bass.ds(layer * NE + s, 1)].rearrange("a p n -> (a p) n")
                                 ).then_inc(expert_in[s], 16)
            return read

        with nc.Fori(0, L) as layer:
            normalised("norm1", read_layer_params(layer), PP_GMIX, sem)
            mix(layer)
            merge(layer)
            normalised("norm2", read_first_experts(layer), PP_GFFN, sem)
            experts(layer)
            first, last = min(layer_sems), max(layer_sems)
            assert last - first + 1 == len(layer_sems)
            nc.gpsimd.sem_clear(range(first, last + 1))
            nc.all_engine_barrier()
        normalised("final", lambda sp: sp.dma_start(reg_a[:, 3 * D:4 * D], fin_in[0:1, :].to_broadcast([P, D])
                                                    ).then_inc(inputs_in, 16), None, once)


def constants():
    c = np.zeros((P, C_N), np.float32)
    c[:, C_ID:C_ID + P] = np.eye(P)
    p = np.arange(P)
    inv = np.float32(10000.0) ** (-np.arange(0, HD // 2, 2, dtype=np.float32) / np.float32(HD // 2))
    for tile in range(T):
        tok = (tile - GROUPS[tile_group(tile)][0]) * P + p
        pos = np.stack([tok // GRID, tok % GRID], -1).astype(np.float32)
        ang = (pos[:, :, None] * inv.astype(np.float32)).astype(np.float32)
        cos, sin = np.cos(ang), np.sin(ang)
        c[:, C_COS + HD * tile:C_COS + HD * (tile + 1)] = np.concatenate([cos, cos], -1).reshape(P, HD)
        c[:, C_SIN + HD * tile:C_SIN + HD * (tile + 1)] = np.concatenate([-sin, sin], -1).reshape(P, HD)
    q, k = (p % GRID)[:, None], np.arange(GRID)[None]
    start = np.clip(q - 8, 0, GRID - 16)
    c[:, C_WIN:C_WIN + GRID] = np.where((k >= start) & (k < start + 16), 0.0, NEG)
    s, t = p[:, None], p[None]
    c[:, C_TRI:C_TRI + P] = np.where(s > t, -NEG, 0.0)
    c[:, C_TRI + P:C_TRI + 2 * P] = np.where(s < t, -NEG, 0.0)
    c[:, C_IOTA:C_IOTA + SPARE] = np.arange(SPARE)
    c[:, C_E128:C_E128 + NE] = P * np.arange(NE)
    c[:, C_BEFORE:C_BEFORE + P] = p[:, None] < p[None]
    return c


def laid_out(a):
    kp = lambda w: np.moveaxis(w.reshape(w.shape[0], KD, P, -1), 1, 2).reshape(w.shape[0], P, -1)
    w = a["w_in"]
    na, ml, gt, cv, at = 0, 768, 768 + 1024, 768 + 1040, 768 + 1040 + 512
    last = np.zeros((L, D, 512), w.dtype)
    last[:, :, 0:BW] = w[:, :, ml + 768:ml + 1024]
    pp = np.zeros((L, P, PP_N), w.dtype)
    for row, src in ((0, 0), (64, 4), (32, 8), (96, 12)):
        last[:, :, BW + row:BW + row + 4] = w[:, :, gt + src:gt + src + 4]
        pp[:, row:row + 4, PP_GB] = a["ml_gate_b"].reshape(L, 16)[:, src:src + 4]
    gate = a["w_gate"].reshape(L, D, NBR, KD, P)
    att_q = w[:, :, at:at + BW].reshape(L, D, 2, 2, HD).transpose(0, 1, 3, 2, 4).reshape(L, D, BW)
    chunks = {"cv": w[:, :, cv:cv + 512], "at": np.concatenate([att_q, w[:, :, at + BW:at + 512]], 2),
              "na": w[:, :, na:na + 512], "ml": w[:, :, ml:ml + 512], "mo": last,
              "nv": np.concatenate([w[:, :, na + 512:na + 768], w[:, :, ml + 512:ml + 768]], 2)}
    chunks |= {f"gate{m}": gate[:, :, :, m].reshape(L, D, 512) for m in range(KD)}
    chunks |= {f"out{c}": a["w_out"][:, :, c * 512:(c + 1) * 512] for c in range(2)}
    wd = np.stack([kp(chunks[name]) for name in CHUNK_NAMES], 1).reshape(L * CHUNKS, P, CW)
    wb = a["w_branch"].reshape(L, NBR, 2, P, 2, 512).transpose(0, 4, 3, 1, 2, 5).reshape(L * 2, P, CW)
    w13 = np.concatenate([a["moe_w1"], a["moe_w3"]], 3).reshape(L * NE, D, 2 * DE)
    w2 = a["moe_w2"].reshape(L * NE, 2, P, D).transpose(0, 2, 1, 3).reshape(L * NE, P, 2 * D)
    we = np.concatenate([kp(w13), w2], 2)
    wr = kp(np.concatenate([a["moe_w_group"], a["moe_w_expert"].reshape(L, D, NE)], 2))
    turned = lambda v, n: v.reshape(L, n, P).transpose(0, 2, 1)
    pp[:, :, PP_GMIX:PP_GMIX + KD] = turned(a["norm_mix_g"], KD)
    pp[:, :, PP_GFFN:PP_GFFN + KD] = turned(a["norm_ffn_g"], KD)
    pp[:, :, PP_CW:PP_CW + 2 * TAPS] = a["conv_dw_w"].reshape(L, TAPS, 2, P).transpose(0, 3, 2, 1).reshape(L, P, -1)
    pp[:, :, PP_CB:PP_CB + 2] = turned(a["conv_dw_b"], 2)
    pp[:, :, PP_BG:PP_BG + 32] = a["b_gate"].reshape(L, NBR, KD, P).transpose(0, 3, 2, 1).reshape(L, P, 32)
    rows = np.concatenate([np.tile(a["att_q_norm_g"], (1, HEADS)), np.tile(a["att_k_norm_g"], (1, 2)), a["ml_norm_g"],
                           a["conv_norm_g"], a["conv_norm_b"], a["moe_b_group"],
                           a["moe_b_expert"].reshape(L, NE)], 1)
    c = np.arange(GRID)
    off = np.clip(c[None, :] - c[:, None] + 15, 0, 30)
    side = np.arange(2)[:, None]
    r = np.clip(np.arange(16)[None] - side, 0, 14)
    bias = a["na_rpb"][:, :, r[:, :, None, None], off[None, None]]
    bias = bias.transpose(0, 2, 4, 1, 3, 5).reshape(L, P, CW)
    return dict(x_prompt=a["x_prompt"], x_sample=a["x_sample"], wd=wd, wb=wb, we=we, wr=wr, pp=pp, rows=rows,
                fin=a["final_norm_g"].reshape(1, D), bias=bias, ffn=a["norm_ffn_g"], consts=constants())


def kernel(**inputs):
    import concourse.bacc as bacc
    from concourse.bass_utils import run_bass_kernel_spmd

    nc = bacc.Bacc("TRN2", target_bir_lowering=False, num_devices=1)
    arrays, args = {}, []
    for name, a in laid_out({k: np.asarray(v) for k, v in inputs.items()}).items():
        a = np.ascontiguousarray(a)
        arrays[f"in_{name}"] = a
        args.append(nc.dram_tensor(f"in_{name}", a.shape, mybir.dt.from_np(a.dtype), kind="ExternalInput").ap())
    args.append(nc.dram_tensor("gate_dram", (KD * NBR, P, TOK), F32, kind="Internal").ap())
    args.append(nc.dram_tensor("blocks", (BLOCKS * P, D), F32, kind="Internal").ap())
    outs = {"y_prompt": (1, 256, D), "y_sample": (1, 512, D)}
    for name, shape in outs.items():
        args.append(nc.dram_tensor(name, shape, F32, kind="ExternalOutput").ap())
    program(nc, *args)
    r = run_bass_kernel_spmd(nc, [arrays], core_ids=[0])
    return tuple(r.results[0][name] for name in outs)
```
